# Optimizing a Trainium2 kernel written in Bass

```python
import jax, jax.numpy as jnp
from jax import lax
import numpy as np

D_MODEL = 1024
BATCH = 1
SEQ = 1024
DEPTH = 1
DEC_BATCH = 8
DEC_SEQ = 1
PAST_LEN = 2048
PAGE_SIZE = 128

N_HEADS = 8
HEAD_DIM = 64
ATTN_WIDTH = N_HEADS * HEAD_DIM
IDX_HEADS = 4
IDX_DIM = 64
TOPK_MAX = 256
QUERY_BLOCK = 128
ROPE_THETA = 500000.0
ROPE_FRACTION = 4
CHUNK = 128
GMLP_GROUPS = 4
GMLP_WIDTH = D_MODEL // 2
N_GROUPS = 4
EXPERTS_PER_GROUP = 8
EXPERT_DIM = D_MODEL // 4
TOP_K_IN_GROUP = 2
LN_EPS = 1e-5
DEEPNORM_ALPHA = (2 * DEPTH) ** 0.25
DEEPNORM_BETA = (8 * DEPTH) ** -0.25
NEG_INF = -1e30

kernel_name = 'hybrid_dsa_gmlp_hmoe_decode_step'

def _proj_sizes():
    return [ATTN_WIDTH, ATTN_WIDTH, ATTN_WIDTH, IDX_HEADS * IDX_DIM, IDX_DIM, IDX_HEADS,
            GMLP_WIDTH, GMLP_WIDTH, D_MODEL, D_MODEL]

def layer_norm(x, g, b):
    xf = x.astype(jnp.float32)
    mu = jnp.mean(xf, axis=-1, keepdims=True)
    var = jnp.mean(jnp.square(xf - mu), axis=-1, keepdims=True)
    y = (xf - mu) * lax.rsqrt(var + LN_EPS) * g.astype(jnp.float32) + b.astype(jnp.float32)
    return y.astype(x.dtype)

def rope_partial(x, pos):
    rot = x.shape[-1] // ROPE_FRACTION
    half = rot // 2
    inv_freq = jnp.power(jnp.float32(ROPE_THETA), -jnp.arange(0, rot, 2, dtype=jnp.float32) / rot)
    ang = pos.astype(jnp.float32)[:, None] * inv_freq[None, :]
    cos = jnp.cos(ang)[None, :, None, :]
    sin = jnp.sin(ang)[None, :, None, :]
    xr = x[..., :rot].astype(jnp.float32)
    x1, x2 = xr[..., :half], xr[..., half:]
    rotated = jnp.concatenate([x1 * cos - x2 * sin, x2 * cos + x1 * sin], axis=-1).astype(x.dtype)
    return jnp.concatenate([rotated, x[..., rot:]], axis=-1)

def project_inputs(x, pos, w_in, gate_bias):
    B, T, _ = x.shape
    offsets = [int(o) for o in np.cumsum(_proj_sizes())[:-1]]
    z = x @ w_in
    q, k, v, qi, ki, wi, u, vb, ga, gb = jnp.split(z, offsets, axis=-1)
    q = rope_partial(q.reshape(B, T, N_HEADS, HEAD_DIM), pos)
    k = rope_partial(k.reshape(B, T, N_HEADS, HEAD_DIM), pos)
    v = v.reshape(B, T, N_HEADS, HEAD_DIM)
    qi = rope_partial(qi.reshape(B, T, IDX_HEADS, IDX_DIM), pos)
    ki = rope_partial(ki[:, :, None, :], pos)[:, :, 0, :]
    ga = jax.nn.sigmoid(ga + gate_bias[0])
    gb = jax.nn.sigmoid(gb + gate_bias[1])
    return q, k, v, qi, ki, wi, u, vb, ga, gb

def index_scores(qi, wi, ki):
    dots = jnp.einsum('bthd,bsd->bths', qi, ki).astype(jnp.float32)
    scale = (IDX_DIM ** -0.5) * (IDX_HEADS ** -0.5)
    return jnp.einsum('bths,bth->bts', jax.nn.relu(dots), wi.astype(jnp.float32)) * scale

def take_rows(rows, idx):
    return jax.vmap(lambda r, i: r[i])(rows, idx)

def sparse_attend(q, ks, vs, valid):
    logits = jnp.einsum('bthd,btkhd->bthk', q, ks).astype(jnp.float32) * (HEAD_DIM ** -0.5)
    logits = jnp.where(valid[:, :, None, :], logits, NEG_INF)
    p = jax.nn.softmax(logits, axis=-1).astype(vs.dtype)
    out = jnp.einsum('bthk,btkhd->bthd', p, vs)
    return out.reshape(out.shape[0], out.shape[1], ATTN_WIDTH)

def prompt_attention(q, k, v, qi, ki, wi):
    B, S = q.shape[0], q.shape[1]
    topk = min(TOPK_MAX, S // 4)
    nblk = S // QUERY_BLOCK
    key_pos = jnp.arange(S)

    def to_blocks(a):
        return jnp.swapaxes(a.reshape((B, nblk, QUERY_BLOCK) + a.shape[2:]), 0, 1)

    def one_block(args):
        qb, qib, wib, start = args
        qpos = start + jnp.arange(QUERY_BLOCK)
        sc = index_scores(qib, wib, ki)
        sc = jnp.where(key_pos[None, None, :] <= qpos[None, :, None], sc, -jnp.inf)
        _, idx = lax.top_k(sc, topk)
        valid = idx <= qpos[None, :, None]
        return sparse_attend(qb, take_rows(k, idx), take_rows(v, idx), valid)

    starts = jnp.arange(nblk, dtype=jnp.int32) * QUERY_BLOCK
    out = lax.map(one_block, (to_blocks(q), to_blocks(qi), to_blocks(wi), starts))
    return jnp.swapaxes(out, 0, 1).reshape(B, S, ATTN_WIDTH)

def sample_attention(q, k_new, v_new, qi, ki_new, wi, cache_k, cache_v, cache_kidx, page_table):
    DB, T = q.shape[0], q.shape[1]
    past = page_table.shape[1] * PAGE_SIZE
    L = past + T
    topk = min(TOPK_MAX, L // 4)
    ki_past = cache_kidx[page_table].reshape(DB, past, IDX_DIM)
    ki_all = jnp.concatenate([ki_past, ki_new], axis=1)
    qpos = past + jnp.arange(T)
    sc = index_scores(qi, wi, ki_all)
    sc = jnp.where(jnp.arange(L)[None, None, :] <= qpos[None, :, None], sc, -jnp.inf)
    _, idx = lax.top_k(sc, topk)
    valid = idx <= qpos[None, :, None]
    from_past = idx < past
    ip = jnp.minimum(idx, past - 1)
    phys = jax.vmap(lambda pt, i: pt[i // PAGE_SIZE])(page_table, ip)
    off = ip % PAGE_SIZE
    inew = jnp.clip(idx - past, 0, T - 1)
    sel = from_past[..., None, None]
    ks = jnp.where(sel, cache_k[phys, off], take_rows(k_new, inew))
    vs = jnp.where(sel, cache_v[phys, off], take_rows(v_new, inew))
    return sparse_attend(q, ks, vs, valid)

def _spatial_weights(w_spatial):
    return w_spatial * jnp.tril(jnp.ones((CHUNK, CHUNK), w_spatial.dtype))

def gmlp_prompt(u, vb, ln_v_g, ln_v_b, w_spatial, b_spatial):
    B, S, _ = u.shape
    vn = layer_norm(vb, ln_v_g, ln_v_b)
    vr = vn.reshape(B, S // CHUNK, CHUNK, GMLP_GROUPS, GMLP_WIDTH // GMLP_GROUPS)
    mix = jnp.einsum('gts,bcsgd->bctgd', _spatial_weights(w_spatial), vr)
    mix = mix + b_spatial.T[None, None, :, :, None]
    return u * mix.reshape(B, S, GMLP_WIDTH)

def gmlp_sample(u, vb, ln_v_g, ln_v_b, w_spatial, b_spatial):
    B, T, _ = u.shape
    vn = layer_norm(vb, ln_v_g, ln_v_b)
    vr = vn.reshape(B, T, GMLP_GROUPS, GMLP_WIDTH // GMLP_GROUPS)
    ws = _spatial_weights(w_spatial)[:, :T, :T]
    mix = jnp.einsum('gts,bsgd->btgd', ws, vr) + b_spatial[:, :T].T[None, :, :, None]
    return u * mix.reshape(B, T, GMLP_WIDTH), vn

def hierarchical_moe(x, w_router_group, b_router_group, w_router_expert, b_router_expert,
                     w_expert_gate, w_expert_up, w_expert_down):
    xt = x.reshape(-1, D_MODEL)
    lg = (xt @ w_router_group + b_router_group).astype(jnp.float32)
    gsel = jnp.argmax(lg, axis=-1)
    pg = jax.nn.softmax(lg, axis=-1)
    pgsel = jnp.take_along_axis(pg, gsel[:, None], axis=-1)[:, 0]
    le = jnp.einsum('td,gde->tge', xt, w_router_expert) + b_router_expert[None]
    le_sel = jnp.take_along_axis(le, gsel[:, None, None], axis=1)[:, 0].astype(jnp.float32)
    vals, eidx = lax.top_k(le_sel, TOP_K_IN_GROUP)
    pw = jax.nn.softmax(vals, axis=-1) * pgsel[:, None]
    comb = jnp.sum(jax.nn.one_hot(eidx, EXPERTS_PER_GROUP, dtype=jnp.float32) * pw[..., None], axis=1)
    out = jnp.zeros_like(xt)
    for g in range(N_GROUPS):
        wg = (comb * (gsel == g)[:, None].astype(jnp.float32)).astype(xt.dtype)
        hg = jax.nn.silu(jnp.einsum('td,edf->tef', xt, w_expert_gate[g])) * \
            jnp.einsum('td,edf->tef', xt, w_expert_up[g])
        out = out + jnp.einsum('tef,efd->td', hg * wg[:, :, None], w_expert_down[g])
    return out.reshape(x.shape)

def merge_and_channel_mix(x, attn_out, gm_out, ga, gb, w_branch_a, w_branch_b, w_o, ln1_g, ln1_b,
                          w_router_group, b_router_group, w_router_expert, b_router_expert,
                          w_expert_gate, w_expert_up, w_expert_down, ln2_g, ln2_b):
    merged = ga * (attn_out @ w_branch_a) + gb * (gm_out @ w_branch_b)
    h = layer_norm(DEEPNORM_ALPHA * x + merged @ w_o, ln1_g, ln1_b)
    f = hierarchical_moe(h, w_router_group, b_router_group, w_router_expert, b_router_expert,
                         w_expert_gate, w_expert_up, w_expert_down)
    return layer_norm(DEEPNORM_ALPHA * h + f, ln2_g, ln2_b)

def setup_inputs(seed: int = 0) -> dict:
    key = jax.random.key(seed)
    ks = jax.random.split(key, 32)
    f32 = jnp.float32
    n_pages = PAST_LEN // PAGE_SIZE
    n_used = DEC_BATCH * n_pages
    n_pool = n_used + n_used // 4

    def nrm(k, shape, scale):
        return jax.random.normal(k, shape, f32) * scale

    sizes = _proj_sizes()
    col_scale = jnp.concatenate([jnp.full((s,), DEEPNORM_BETA if i == 2 else 1.0, f32)
                                 for i, s in enumerate(sizes)])
    return {
        'x_prompt': nrm(ks[0], (BATCH, SEQ, D_MODEL), 1.0),
        'x_sample': nrm(ks[1], (DEC_BATCH, DEC_SEQ, D_MODEL), 1.0),
        'cache_k': nrm(ks[2], (n_pool, PAGE_SIZE, N_HEADS, HEAD_DIM), 1.0),
        'cache_v': nrm(ks[3], (n_pool, PAGE_SIZE, N_HEADS, HEAD_DIM), 1.0),
        'cache_kidx': nrm(ks[4], (n_pool, PAGE_SIZE, IDX_DIM), 1.0),
        'page_table': jax.random.permutation(ks[5], n_pool)[:n_used].reshape(DEC_BATCH, n_pages).astype(jnp.int32),
        'w_in': nrm(ks[6], (D_MODEL, sum(sizes)), D_MODEL ** -0.5) * col_scale[None, :],
        'gate_bias': nrm(ks[7], (2, D_MODEL), 0.1),
        'ln_v_g': 1.0 + nrm(ks[8], (GMLP_WIDTH,), 0.05),
        'ln_v_b': nrm(ks[9], (GMLP_WIDTH,), 0.05),
        'w_spatial': nrm(ks[10], (GMLP_GROUPS, CHUNK, CHUNK), CHUNK ** -0.5),
        'b_spatial': 1.0 + nrm(ks[11], (GMLP_GROUPS, CHUNK), 0.1),
        'w_branch_a': nrm(ks[12], (ATTN_WIDTH, D_MODEL), ATTN_WIDTH ** -0.5 * DEEPNORM_BETA),
        'w_branch_b': nrm(ks[13], (GMLP_WIDTH, D_MODEL), GMLP_WIDTH ** -0.5 * DEEPNORM_BETA),
        'w_o': nrm(ks[14], (D_MODEL, D_MODEL), D_MODEL ** -0.5 * DEEPNORM_BETA),
        'ln1_g': 1.0 + nrm(ks[15], (D_MODEL,), 0.05),
        'ln1_b': nrm(ks[16], (D_MODEL,), 0.05),
        'w_router_group': nrm(ks[17], (D_MODEL, N_GROUPS), D_MODEL ** -0.5),
        'b_router_group': nrm(ks[18], (N_GROUPS,), 0.01),
        'w_router_expert': nrm(ks[19], (N_GROUPS, D_MODEL, EXPERTS_PER_GROUP), D_MODEL ** -0.5),
        'b_router_expert': nrm(ks[20], (N_GROUPS, EXPERTS_PER_GROUP), 0.01),
        'w_expert_gate': nrm(ks[21], (N_GROUPS, EXPERTS_PER_GROUP, D_MODEL, EXPERT_DIM), D_MODEL ** -0.5),
        'w_expert_up': nrm(ks[22], (N_GROUPS, EXPERTS_PER_GROUP, D_MODEL, EXPERT_DIM), D_MODEL ** -0.5),
        'w_expert_down': nrm(ks[23], (N_GROUPS, EXPERTS_PER_GROUP, EXPERT_DIM, D_MODEL), EXPERT_DIM ** -0.5 * DEEPNORM_BETA),
        'ln2_g': 1.0 + nrm(ks[24], (D_MODEL,), 0.05),
        'ln2_b': nrm(ks[25], (D_MODEL,), 0.05),
    }

def reference(x_prompt, x_sample, cache_k, cache_v, cache_kidx, page_table, w_in, gate_bias,
              ln_v_g, ln_v_b, w_spatial, b_spatial, w_branch_a, w_branch_b, w_o, ln1_g, ln1_b,
              w_router_group, b_router_group, w_router_expert, b_router_expert,
              w_expert_gate, w_expert_up, w_expert_down, ln2_g, ln2_b):
    pos_p = jnp.arange(x_prompt.shape[1], dtype=jnp.int32)
    qp, kp, vp, qip, kip, wip, up, vbp, gap, gbp = project_inputs(x_prompt, pos_p, w_in, gate_bias)
    attn_p = prompt_attention(qp, kp, vp, qip, kip, wip)
    gm_p = gmlp_prompt(up, vbp, ln_v_g, ln_v_b, w_spatial, b_spatial)
    y_prompt = merge_and_channel_mix(x_prompt, attn_p, gm_p, gap, gbp, w_branch_a, w_branch_b, w_o,
                                     ln1_g, ln1_b, w_router_group, b_router_group, w_router_expert,
                                     b_router_expert, w_expert_gate, w_expert_up, w_expert_down,
                                     ln2_g, ln2_b)
    past = page_table.shape[1] * PAGE_SIZE
    pos_s = past + jnp.arange(x_sample.shape[1], dtype=jnp.int32)
    qs, ks, vs, qis, kis, wis, us, vbs, gas, gbs = project_inputs(x_sample, pos_s, w_in, gate_bias)
    attn_s = sample_attention(qs, ks, vs, qis, kis, wis, cache_k, cache_v, cache_kidx, page_table)
    gm_s, chunk_v_s = gmlp_sample(us, vbs, ln_v_g, ln_v_b, w_spatial, b_spatial)
    y_sample = merge_and_channel_mix(x_sample, attn_s, gm_s, gas, gbs, w_branch_a, w_branch_b, w_o,
                                     ln1_g, ln1_b, w_router_group, b_router_group, w_router_expert,
                                     b_router_expert, w_expert_gate, w_expert_up, w_expert_down,
                                     ln2_g, ln2_b)
    return (y_prompt, y_sample, kp, vp, kip, ks, vs, kis, chunk_v_s)


_drawn_inputs = setup_inputs


def setup_inputs(seed=0):
    import zlib

    import numpy as np

    out = dict(_drawn_inputs(seed))
    spreads = {}
    factors = {'cache_k': 3.297,
     'cache_v': 3.464,
     'cache_kidx': 3.758,
     'gate_bias': 4.309,
     'w_branch_a': 3.381,
     'b_router_expert': 6.072}
    for name, (base, spread) in spreads.items():
        noise = np.random.default_rng([zlib.crc32(name.encode()), seed]).standard_normal(out[name].shape)
        drawn = base * np.exp(spread * noise) if base else spread * noise
        out[name] = __import__('jax').numpy.asarray(drawn.astype(out[name].dtype))
    for name, factor in factors.items():
        out[name] = (out[name] * factor).astype(out[name].dtype)
    return out
```

```python
from contextlib import ExitStack

import numpy as np
import concourse.bass as bass
from concourse import mybir

F32 = mybir.dt.float32
BF16 = mybir.dt.bfloat16
I32 = mybir.dt.int32
U32 = mybir.dt.uint32
ALU = mybir.AluOpType
ACT = mybir.ActivationFunctionType
AX = mybir.AxisListType

P = 128
D = 1024
KC = D // P
SEQ = 1024
N_SAMPLE = 8
NT = SEQ // P
TILES = NT + 1
TOK = TILES * P
HEADS = 8
HD = 64
AW = HEADS * HD
IDX_HEADS = 4
ROT_HALF = HD // 4 // 2
W_QKVI = 3 * AW + IDX_HEADS * HD + HD + IDX_HEADS
IDX0 = 3 * AW
ROPE_HEADS = 2 * HEADS + IDX_HEADS + 1
ZW = (ROPE_HEADS + 1) * HD
PAST = 2048
PAGES = PAST // P
GW = 512
GROUPS = 4
BUFS = 3
TOPK = 256
ROUNDS = TOPK // 8
TAKEN = -3.0e38
HIDDEN = -1.0e38
NEG = -1.0e30
ALPHA = 2.0 ** 0.25
EPS = 1e-5


class Chain:

    def __init__(self, eng, sem, start=0):
        self.eng, self.sem, self.n = eng, sem, start

    def __call__(self, ins, wait=True):
        ins.then_inc(self.sem, 1)
        self.n = self.n + 1
        if wait:
            self.eng.wait_ge(self.sem, self.n)


def project(nc, ins, outs, keep):
    with nc.cleanup_on_exit(), ExitStack() as ctx:
        def sb(name, shape, dt=F32):
            return ctx.enter_context(nc.sbuf_tensor(name, shape, dt))

        def sem(name):
            return nc.alloc_semaphore(name)

        w = sb("w_qkvi", [P, KC, W_QKVI])
        x = [sb(f"xT{j}", [P, KC, P]) for j in range(BUFS)]
        z = [sb(f"z{j}", [P, ZW]) for j in range(BUFS)]
        rot = sb("rot", [P, TILES, 2, ROT_HALF])
        tmp = sb("rope_tmp", [P, 4, ROPE_HEADS, ROT_HALF])
        ident = keep["ident"]
        acc = [ctx.enter_context(nc.psum_tensor(f"acc{b}", [P, 512], F32)) for b in range(4)]
        turned = [ctx.enter_context(nc.psum_tensor(f"turned{b}", [P, 512], F32)) for b in range(3)]
        cols = [(0, AW), (AW, 2 * AW), (IDX0, W_QKVI), (2 * AW, 3 * AW)]

        x_in = [sem(f"x_in{j}") for j in range(BUFS)]
        w_in = [sem(f"w_in{k}") for k in range(KC)]
        const_in = sem("const_in")
        acc_full = sem("acc_full")
        acc_read = sem("acc_read")
        roped = sem("roped")
        turned_full = sem("turned_full")
        turned_read = sem("turned_read")
        stored = [sem(f"stored{j}") for j in range(BUFS)]
        dve_step = sem("dve_step")
        table_in = sem("table_in")
        kidx_in = sem("kidx_in")

        block = ctx.enter_context(nc.Block())
        iters = TILES // BUFS

        @block.gpsimd
        def _(pool):
            pool.dma_start(keep["table"][:], ins["page_table"]).then_inc(table_in, 16)
            pool.wait_ge(table_in, 16)
            half_pages = N_SAMPLE // 2 * PAGES
            for odd in range(2):
                with pool.Fori(0, half_pages) as n:
                    page = pool.value_load(keep["table"][0:1, bass.ds(n + odd * half_pages, 1)],
                                           min_val=0, max_val=ins["kidx_pool"].shape[0] - 1)
                    pool.dma_start(keep["kidx"][odd * HD:(odd + 1) * HD, bass.ds(n * P, P)],
                                   ins["kidx_pool"][bass.ds(page, 1)]).then_inc(kidx_in, 16)
            pool.wait_ge(kidx_in, 16 * N_SAMPLE * PAGES)

        @block.sync
        def _(sp):
            for k in range(KC):
                sp.dma_start(w[:, k, :], ins["w_qkvi"][k]).then_inc(w_in[k], 16)
                if k < BUFS:
                    sp.dma_start(x[k][:], ins["x_tiles"][k]).then_inc(x_in[k], 16)
                if k == 0:
                    sp.dma_start(rot[:], ins["rot"]).then_inc(const_in, 16)
                    sp.dma_start(ident[:], ins["ident"]).then_inc(const_in, 16)

            def store_and_reload(i, reload):
                for j in range(BUFS):
                    t = i * BUFS + j
                    sp.wait_ge(roped, t + 1)
                    sp.dma_start(outs["k_all"][bass.ds(t, 1)], z[j][:, AW:2 * AW]).then_inc(stored[j], 16)
                    sp.dma_start(outs["kidx_all"][bass.ds(t, 1)],
                                 z[j][:, (ROPE_HEADS - 1) * HD:ROPE_HEADS * HD]).then_inc(stored[j], 16)
                    sp.wait_ge(acc_read, t * 5 + 10)
                    sp.dma_start(outs["v_all"][bass.ds(t, 1)], keep["v"][:, bass.ds(t, 1), :]).then_inc(stored[j], 16)
                    if reload:
                        sp.wait_ge(acc_full, t * 4 + 4)
                        sp.dma_start(x[j][:], ins["x_tiles"][bass.ds(t + BUFS, 1)]).then_inc(x_in[j], 16)

            with sp.Fori(0, iters - 1) as i:
                store_and_reload(i, True)
            store_and_reload(iters - 1, False)
            for j in range(BUFS):
                sp.wait_ge(stored[j], 48 * iters)

        @block.tensor
        def _(pe):
            pe.wait_ge(const_in, 32)
            for k in range(KC):
                pe.wait_ge(w_in[k], 16)
            with pe.Fori(0, iters) as i:
                for j in range(BUFS):
                    t = i * BUFS + j
                    pe.wait_ge(x_in[j], i * 16 + 16)
                    for b, (c0, c1) in enumerate(cols):
                        pe.wait_ge(acc_read, t * 5 + (1, 2, 4, 5)[b])
                        for k in range(KC):
                            mm = nc.tensor.matmul(acc[b][:, 0:c1 - c0], x[j][:, k, :], w[:, k, c0:c1],
                                                  start=(k == 0), stop=(k == KC - 1))
                        mm.then_inc(acc_full, 1)
                    pe.wait_ge(roped, t + 1)
                    for b, heads in enumerate((range(0, HEADS, 2), range(HEADS, 2 * HEADS, 2),
                                               range(2 * HEADS, ROPE_HEADS + 1, 2))):
                        pe.wait_ge(turned_read, t * 3 + b + 1)
                        for n, h in enumerate(heads):
                            mm = nc.tensor.transpose(turned[b][:, n * P:(n + 1) * P],
                                                     z[j][:, h * HD:(h + 2) * HD], ident[:])
                        mm.then_inc(turned_full, 1)

        @block.scalar
        def _(act):
            act.sem_inc(acc_read, 5)
            with act.Fori(0, iters) as i:
                for j in range(BUFS):
                    t = i * BUFS + j
                    act.wait_ge(acc_full, t * 4 + 1)
                    act.wait_ge(stored[j], i * 48)
                    nc.scalar.copy(z[j][:, 0:AW], acc[0][:]).then_inc(acc_read, 1)
                    act.wait_ge(acc_full, t * 4 + 2)
                    nc.scalar.copy(z[j][:, AW:2 * AW], acc[1][:]).then_inc(acc_read, 1)
                    act.wait_ge(acc_full, t * 4 + 3)
                    nc.scalar.copy(z[j][:, 2 * AW:ROPE_HEADS * HD], acc[2][:, 0:W_QKVI - IDX0 - IDX_HEADS]).then_inc(acc_read, 1)
                    nc.scalar.mul(keep["wi"][:, bass.ds(t, 1), :], acc[2][:, W_QKVI - IDX0 - IDX_HEADS:W_QKVI - IDX0],
                                  HD ** -0.5 * IDX_HEADS ** -0.5).then_inc(acc_read, 1)
                    act.wait_ge(acc_full, t * 4 + 4)
                    nc.scalar.copy(keep["v"][:, bass.ds(t, 1), :], acc[3][:]).then_inc(acc_read, 1)

        @block.vector
        def _(dve):
            dve.sem_inc(turned_read, 3)
            dve.wait_ge(const_in, 32)
            per_tile = 6
            with dve.Fori(0, iters) as i:
                for j in range(BUFS):
                    t = i * BUFS + j
                    step = Chain(dve, dve_step, t * per_tile)
                    zh = z[j][:, 0:ROPE_HEADS * HD].rearrange("p (h d) -> p h d", d=HD)
                    x1, x2 = zh[:, :, 0:ROT_HALF], zh[:, :, ROT_HALF:2 * ROT_HALF]
                    cos, sin = (rot[:, bass.ds(t, 1), c, :].to_broadcast([P, ROPE_HEADS, ROT_HALF]) for c in (0, 1))
                    dve.wait_ge(acc_read, t * 5 + 8)
                    step(nc.vector.tensor_tensor(tmp[:, 0], x1, cos, ALU.mult), wait=False)
                    step(nc.vector.tensor_tensor(tmp[:, 1], x2, sin, ALU.mult), wait=False)
                    step(nc.vector.tensor_tensor(tmp[:, 2], x2, cos, ALU.mult), wait=False)
                    step(nc.vector.tensor_tensor(tmp[:, 3], x1, sin, ALU.mult))
                    step(nc.vector.tensor_tensor(x1, tmp[:, 0], tmp[:, 1], ALU.subtract), wait=False)
                    step(nc.vector.tensor_tensor(x2, tmp[:, 2], tmp[:, 3], ALU.add))
                    nc.vector.tensor_copy(z[j][:, ROPE_HEADS * HD:ZW],
                                          z[j][:, (ROPE_HEADS - 1) * HD:ROPE_HEADS * HD]).then_inc(roped, 1)
                    for b, name in enumerate(("qT", "kT")):
                        dve.wait_ge(turned_full, t * 3 + b + 1)
                        nc.vector.tensor_copy(keep[name][:, :, bass.ds(t * P, P)],
                                              turned[b][:].rearrange("p (n q) -> p n q", q=P)).then_inc(turned_read, 1)
                    dve.wait_ge(turned_full, t * 3 + 3)
                    nc.vector.tensor_copy(keep["qkiT"][:, :, bass.ds(t * P, P)],
                                          turned[2][:, 0:3 * P].rearrange("p (n q) -> p n q", q=P)).then_inc(turned_read, 1)


def wait_alone(eng, sem, value, idle):
    eng.wait_ge(sem, value)
    eng.sem_inc(idle, 1)


def staggered(eng, n, stages, par=2):
    deep = max(d for d, _ in stages)

    def at(s, j, runs):
        for d, work in stages:
            if runs(d):
                work(s - d, (j - d) % par)

    whole = (n - deep) // par
    for s in range(deep):
        at(s, s, lambda d: s - d >= 0)
    if whole:
        with eng.Fori(0, whole) as i:
            for j in range(par):
                at(i * par + (deep + j), deep + j, lambda d: True)
    for s in range(deep + whole * par, n + deep):
        at(s, s, lambda d: s - d < n)


def index_scores(nc, ins, outs, keep):
    BH = N_SAMPLE * IDX_HEADS
    with nc.cleanup_on_exit(), ExitStack() as ctx:
        def sb(name, shape, dt=F32):
            return ctx.enter_context(nc.sbuf_tensor(name, shape, dt))

        def sem(name):
            return nc.alloc_semaphore(name)

        ident, wi, qki, score, score_s = (keep[n] for n in ("ident", "wi", "qkiT", "score", "score_s"))
        ps = ctx.enter_context(nc.psum_tensor("ps_index", [P, 8, 512], F32))
        relu = [sb(f"relu{j}", [P, SEQ]) for j in range(2)]
        cap = sb("causal_cap", [P, P])
        kidx = keep["kidx"]
        PAIRS = N_SAMPLE // 2
        qi_diag = sb("qi_diag", [P, PAIRS * (BH + 2 * IDX_HEADS)])
        ki_own = sb("ki_own", [P, PAIRS])
        delta = sb("delta", [N_SAMPLE, N_SAMPLE])
        wi_rows = sb("wi_rows", [N_SAMPLE, N_SAMPLE, IDX_HEADS])
        wi_diag = sb("wi_diag", [BH, N_SAMPLE])
        relu_s = sb("relu_s", [BH, PAST + 1])

        const_in = sem("i_const_in")
        picked = sem("qi_picked")
        diag_ready = sem("qi_diag_ready")
        wi_turned = sem("wi_turned")
        dots = sem("dots")
        rectified = sem("rectified")
        summed = sem("heads_summed")
        scored = sem("scored")
        score_read = sem("score_read")
        dve_step = sem("i_dve_step")
        units = [(t, h) for t in range(TOPK // P, NT) for h in range(IDX_HEADS)]

        block = ctx.enter_context(nc.Block())

        @block.sync
        def _(sp):
            sp.dma_start(cap[:], ins["causal_cap"]).then_inc(const_in, 16)
            sp.dma_start(delta[:], ins["ident"][0:N_SAMPLE, 0:N_SAMPLE]).then_inc(const_in, 16)

        @block.tensor
        def _(pe):
            for h, to in ((h, to) for h in range(IDX_HEADS) for to in (0, HD)):
                half = (h % 2) * HD
                mm = nc.tensor.matmul(ps[to:to + HD, 7, h * N_SAMPLE:(h + 1) * N_SAMPLE], ident[:, half:half + HD],
                                      qki[:, h // 2, SEQ:SEQ + N_SAMPLE], start=True, stop=True)
            mm.then_inc(picked, 1)
            pe.wait_ge(diag_ready, 3)
            nc.tensor.transpose(ps[0:BH, 6, 0:N_SAMPLE], wi_rows[:].rearrange("a b h -> a (b h)"),
                                ident[0:N_SAMPLE, 0:N_SAMPLE]).then_inc(wi_turned, 1)
            for n, (t, h) in enumerate(units):
                if n >= 2:
                    pe.wait_ge(rectified, n - 1)
                half = (h % 2) * HD
                width = (t + 1) * P
                for c in range(0, width, 512):
                    c1 = min(width, c + 512)
                    mm = nc.tensor.matmul(ps[:, 2 * (n % 2) + c // 512, 0:c1 - c],
                                          qki[half:half + HD, h // 2, t * P:(t + 1) * P],
                                          qki[half:half + HD, 2, c:c1], start=True, stop=True)
                mm.then_inc(dots, 1)
            pe.wait_ge(diag_ready, 4)
            pe.wait_ge(rectified, len(units))
            for i in range(PAIRS):
                for c in range(4):
                    nc.tensor.matmul(ps[0:BH, c, :], qi_diag[:, i * BH:(i + 1) * BH],
                                     kidx[:, i * PAST + c * 512:i * PAST + (c + 1) * 512],
                                     start=(i == 0), stop=(i == PAIRS - 1))
            for i in range(PAIRS):
                mm = nc.tensor.matmul(ps[0:BH, 4, 0:1], qi_diag[:, i * BH:(i + 1) * BH], ki_own[:, i:i + 1],
                                      start=(i == 0), stop=(i == PAIRS - 1))
            mm.then_inc(dots, 1)
            for c in range(5):
                pe.wait_ge(rectified, len(units) + 5)
                width = 512 if c < 4 else 1
                mm = nc.tensor.matmul(ps[0:N_SAMPLE, c, 0:width], wi_diag[:], relu_s[:, c * 512:c * 512 + width],
                                      start=True, stop=True)
                mm.then_inc(scored, 1)

        @block.scalar
        def _(act):
            for n, (t, h) in enumerate(units):
                act.wait_ge(dots, n + 1)
                if n >= 2:
                    act.wait_ge(summed, n - 1)
                width = (t + 1) * P
                banks = ps[:, 2 * (n % 2):2 * (n % 2) + 2, :].rearrange("p b c -> p (b c)")
                nc.scalar.activation(relu[n % 2][:, 0:width], banks[:, 0:width], ACT.Relu).then_inc(rectified, 1)
            act.wait_ge(dots, len(units) + 1)
            for c in range(5):
                width = 512 if c < 4 else 1
                nc.scalar.activation(relu_s[:, c * 512:c * 512 + width], ps[0:BH, c, 0:width],
                                     ACT.Relu).then_inc(rectified, 1)
            for c in range(5):
                act.wait_ge(scored, c + 1)
                width = 512 if c < 4 else 1
                nc.scalar.copy(score_s[:, c * 512:c * 512 + width], ps[0:N_SAMPLE, c, 0:width]).then_inc(score_read, 1)

        @block.vector
        def _(dve):
            step = Chain(dve, dve_step)
            step(nc.vector.memset(qi_diag[:], 0.0))
            dve.wait_ge(picked, 1)
            for odd, q0 in enumerate((0, HD)):
                to = qi_diag[q0:q0 + HD, :].rearrange("p (i s) -> p i s", s=BH + 2 * IDX_HEADS)
                own = ps[q0:q0 + HD, 7, 0:BH].rearrange("p (h i two) -> p two i h", h=IDX_HEADS, two=2)
                step(nc.vector.tensor_copy(to[:, :, odd * IDX_HEADS:(odd + 1) * IDX_HEADS], own[:, odd]), wait=False)
                keys = qki[q0:q0 + HD, 2, SEQ:SEQ + N_SAMPLE].rearrange("p (i two) -> p two i", two=2)
                last = nc.vector.tensor_copy(ki_own[q0:q0 + HD, :], keys[:, odd])
                last.then_inc(diag_ready, 1)
            dve.wait_ge(const_in, 32)
            spread = [N_SAMPLE, N_SAMPLE, IDX_HEADS]
            nc.vector.tensor_tensor(wi_rows[:], delta[:].unsqueeze(2).to_broadcast(spread),
                                    wi[0:N_SAMPLE, TILES - 1:TILES, :].to_broadcast(spread),
                                    ALU.mult).then_inc(diag_ready, 1)
            dve.wait_ge(wi_turned, 1)
            nc.vector.tensor_copy(wi_diag[:], ps[0:BH, 6, 0:N_SAMPLE]).then_inc(diag_ready, 1)
            for n, (t, h) in enumerate(units):
                dve.wait_ge(rectified, n + 1)
                r, s, weight = relu[n % 2][:, 0:(t + 1) * P], score[t][:], wi[:, t, h:h + 1]
                if h == 0:
                    last = nc.vector.tensor_scalar(s, r, weight, None, ALU.mult)
                else:
                    dve.wait_ge(summed, n)
                    last = nc.vector.scalar_tensor_tensor(s, r, weight, s, ALU.mult, ALU.add)
                last.then_inc(summed, 1)
                if h == IDX_HEADS - 1:
                    dve.wait_ge(summed, n + 1)
                    step(nc.vector.tensor_tensor(s[:, t * P:], s[:, t * P:], cap[:], ALU.min), wait=False)


PIECES = [(0, 512), (512, 512), (SEQ, N_SAMPLE)]


def choose_keys_and_gate(nc, ins, outs, keep, scratch):
    with nc.cleanup_on_exit(), ExitStack() as ctx:
        def sb(name, shape, dt=F32):
            return ctx.enter_context(nc.sbuf_tensor(name, shape, dt))

        def sem(name):
            return nc.alloc_semaphore(name)

        ident, score, score_s = keep["ident"], keep["score"], keep["score_s"]
        gmT = sb("gmT", [P, GROUPS, SEQ + N_SAMPLE])
        arena = sb("arena", [P, KC * 2 * GW + 2 * KC * P])
        w_uv = arena[:, 0:KC * 2 * GW].rearrange("p (k n) -> p k n", k=KC)
        x = [arena[:, KC * 2 * GW + j * KC * P:KC * 2 * GW + (j + 1) * KC * P].rearrange("p (k n) -> p k n", k=KC)
             for j in range(2)]
        x_all = arena[:, 0:KC * (SEQ + N_SAMPLE)].rearrange("p (k n) -> p k n", k=KC)
        u = [sb(f"u{j}", [P, GW]) for j in range(2)]
        vb = [sb(f"vb{j}", [P, GW]) for j in range(2)]
        mixb = sb("mixb", [P, GW])
        stat = [sb(f"stat{j}", [P, 4]) for j in range(2)]
        minus_half = sb("minus_half", [P, 1])
        ln_v = sb("ln_v", [P, 2, GW])
        w_sp = sb("w_sp", [P, GROUPS, P])
        w00 = sb("w00", [P, GROUPS])
        b_sp = sb("b_sp", [P, 2, GROUPS])
        gate_bias = sb("gate_bias", [P, 2, KC])
        w_gate = [sb(f"w_gate{j}", [P, 2 * KC + GROUPS, P]) for j in range(2)]
        made = [sb(f"made{j}", [P, 3, 512]) for j in range(2)]
        top8 = [sb(f"top8_{j}", [P, 8]) for j in range(2)]
        pages_i = sb("pages_i", [P, N_SAMPLE * PAGES], I32)
        ids = sb("ids", [P, N_SAMPLE, PAGES, 2], BF16)
        rank = sb("rank", [P, TOPK], I32)
        rank_b = sb("rank_b", [P, TOPK], BF16)
        part = sb("part", [P, 1])
        place = sb("place", [P, PAGES, N_SAMPLE])
        counted = arena[0:N_SAMPLE, 0:PAST]
        hot = [arena[:, PAST * (1 + j):PAST * (2 + j)].bitcast(BF16).rearrange("p (g n) -> p g n", g=PAGES)
               for j in range(2)]
        found = sb("found", [P, 2 * N_SAMPLE, 2])
        rows_f = sb("rows_f", [P, 2 * N_SAMPLE])
        ps = ctx.enter_context(nc.psum_tensor("ps_gate", [P, 8, 512], F32))
        U, V, MIX, TURN = 0, 1, 2, 3
        SETS = ((4, 5, 6), (7, 0, 1))

        const_in, w_uv_in, x_all_in = sem("c_const_in"), sem("w_uv_in"), sem("x_all_in")
        x_in = [sem(f"c_x_in{j}") for j in range(2)]
        uv_full = sem("uv_full")
        uv_read = sem("uv_read")
        act_step = sem("act_step")
        pool_step = sem("pool_step")
        masked = sem("w_sp_masked")
        normed = sem("normed")
        mixed = sem("mixed")
        biased = sem("biased")
        gated = sem("gated")
        gm_turned = sem("gm_turned")
        gm_read = sem("gm_read")
        w_gate_in = [sem(f"w_gate_in{j}") for j in range(2)]
        gates_full = sem("gates_full")
        gates_read = sem("gates_read")
        multiplied = sem("multiplied")
        made_out = [sem(f"made_out{j}") for j in range(2)]
        chunk_out = sem("chunk_out")
        taken = sem("taken")
        placed = sem("placed")
        place_turned = sem("place_turned")
        hot_ready = sem("hot_ready")
        hot_used = sem("hot_used")
        idle = [sem(f"idle{n}") for n in range(3)]

        block = ctx.enter_context(nc.Block())
        N_CONST = 11

        @block.sync
        def _(sp):
            sp.dma_start(w_uv, ins["w_uv"]).then_inc(w_uv_in, 16)
            for j in range(2):
                sp.dma_start(x[j], ins["x_tiles"][j]).then_inc(x_in[j], 16)
            for to, name in ((w_sp[:], "w_spatial_t"), (ln_v[:, 0, :], "ln_v_g"), (ln_v[:, 1, :], "ln_v_b"),
                             (w00[:], "w_spatial_00"), (b_sp[:, 0, :], "b_spatial_t"), (b_sp[:, 1, :], "b_spatial_0"),
                             (gate_bias[:], "gate_bias_t"), (part[:], "part_index"), (minus_half[:], "minus_half"),
                             (pages_i[:], "page_table"), (rank[:], "rank")):
                src = ins[name]
                sp.dma_start(to, src.to_broadcast([P, src.shape[1]]) if src.shape[0] == 1 else src).then_inc(const_in, 16)

            def next_x(t, j):
                sp.wait_ge(uv_full, t * 2 - 2)
                sp.dma_start(x[j], ins["x_tiles"][bass.ds(t, 1)]).then_inc(x_in[j], 16)

            for t in range(2, 4):
                next_x(t, t % 2)
            with sp.Fori(2, TILES // 2) as i:
                for j in range(2):
                    next_x(i * 2 + j, j)
            next_x(TILES - 1, (TILES - 1) % 2)
            sp.wait_ge(normed, TILES)
            sp.dma_start(outs["chunk_v"], vb[(TILES - 1) % 2][0:N_SAMPLE, :]).then_inc(chunk_out, 16)
            for j in range(2):
                sp.dma_start(w_gate[j][:], ins["w_gate"][j]).then_inc(w_gate_in[j], 16)
            sp.wait_ge(uv_full, TILES * 2)
            sp.dma_start(x_all, ins["x_all"]).then_inc(x_all_in, 16)

            def store(blk, j, last):
                for p, (c0, n) in enumerate(PIECES):
                    at = j * 3 + p
                    sp.wait_ge(multiplied, (blk - j) * 3 + at + 1)
                    for which, name in ((0, "gate_a"), (1, "merged_b")):
                        sp.dma_start(scratch[name][bass.ds(blk, 1), :, c0:c0 + n],
                                     made[at % 2][:, which, 0:n]).then_inc(made_out[at % 2], 16)
                if not last:
                    sp.wait_ge(gates_full, blk * 9 + 9)
                    sp.dma_start(w_gate[j][:], ins["w_gate"][bass.ds(blk + 2, 1)]).then_inc(w_gate_in[j], 16)

            with sp.Fori(0, KC // 2 - 1) as i:
                for j in range(2):
                    store(i * 2 + j, j, False)
            for j in range(2):
                store(KC - 2 + j, j, True)
            sp.wait_ge(chunk_out, 16)
            for j in range(2):
                sp.wait_ge(made_out[j], 32 * KC * 3 // 2)

        @block.tensor
        def _(pe):
            def make_uv(t, j):
                pe.wait_ge(x_in[j], (t - j) * 8 + 16)
                for b in (U, V):
                    pe.wait_ge(uv_read, t * 2 + b + 1)
                    for k in range(KC):
                        mm = nc.tensor.matmul(ps[:, b, :], x[j][:, k, :], w_uv[:, k, b * GW:(b + 1) * GW],
                                              start=(k == 0), stop=(k == KC - 1))
                    mm.then_inc(uv_full, 1)

            def mix(t, j):
                pe.wait_ge(normed, t + 1)
                if isinstance(t, int) and t == TILES - 1:
                    return
                for g in range(GROUPS):
                    if isinstance(t, int) and t == 0:
                        pass
                    if g == 0:
                        pe.wait_ge(biased, t * GROUPS)
                    mm = nc.tensor.matmul(ps[:, MIX, g * P:(g + 1) * P], w_sp[:, g, :], vb[j][:, g * P:(g + 1) * P],
                                          start=True, stop=True)
                mm.then_inc(mixed, 1)

            def turn(t, j):
                pe.wait_ge(gated, t + 1)
                pe.wait_ge(gm_read, t + 1)
                for g in range(GROUPS):
                    mm = nc.tensor.transpose(ps[:, TURN, g * P:(g + 1) * P], u[j][:, g * P:(g + 1) * P], ident[:])
                mm.then_inc(gm_turned, 1)

            pe.wait_ge(w_uv_in, 16)
            pe.wait_ge(masked, 1)
            staggered(pe, TILES, [(0, make_uv), (1, mix), (2, turn)])
            pe.wait_ge(x_all_in, 16)
            pe.wait_ge(gm_read, TILES + 1)
            with pe.Fori(0, KC // 2) as i:
                for j in range(2):
                    pe.wait_ge(w_gate_in[j], i * 16 + 16)
                    for p, (c0, n) in enumerate(PIECES):
                        at = j * 3 + p
                        for which in range(3):
                            pe.wait_ge(gates_read, i * 18 + at * 3 + which + 1)
                            chunks = KC if which < 2 else GROUPS
                            right = x_all if which < 2 else gmT
                            for k in range(chunks):
                                mm = nc.tensor.matmul(ps[:, SETS[at % 2][which], 0:n],
                                                      w_gate[j][:, which * KC + k, :], right[:, k, c0:c0 + n],
                                                      start=(k == 0), stop=(k == chunks - 1))
                            mm.then_inc(gates_full, 1)
            pe.wait_ge(placed, 1)
            for g in range(PAGES):
                nc.tensor.transpose(ps[:, MIX, g * N_SAMPLE:(g + 1) * N_SAMPLE], score_s[:, g * P:(g + 1) * P],
                                    ident[0:N_SAMPLE, 0:N_SAMPLE])
            nc.tensor.transpose(ps[0:1, MIX, 256:256 + N_SAMPLE], score_s[:, PAST:PAST + 1],
                                ident[0:N_SAMPLE, 0:N_SAMPLE]).then_inc(place_turned, 1)
            with pe.Fori(0, N_SAMPLE // 2) as i:
                for j in range(2):
                    b = i * 2 + j
                    pe.wait_ge(hot_ready, b + 1)
                    for half in range(2):
                        for g in range(PAGES):
                            mm = nc.tensor.matmul(ps[:, TURN, bass.ds(b * 4 + half * 2, 2)],
                                                  hot[j][:, g, half * P:(half + 1) * P],
                                                  ids[:, bass.ds(b, 1), g, :], start=(g == 0), stop=(g == PAGES - 1))
                    mm.then_inc(hot_used, 1)

        @block.scalar
        def _(act):
            act.sem_inc(uv_read, 2)
            act.sem_inc(gm_read, 1)
            act.sem_inc(gates_read, 6)
            act.wait_ge(const_in, 16 * N_CONST)

            def read_uv(t, j):
                act.wait_ge(uv_full, t * 2 + 1)
                if not (isinstance(t, int) and t < 2):
                    act.wait_ge(gm_turned, t - 1)
                nc.scalar.copy(u[j][:], ps[:, U, :]).then_inc(uv_read, 1)
                act.wait_ge(uv_full, t * 2 + 2)
                nc.scalar.activation(vb[j][:], ps[:, V, :], ACT.Copy, accum_out=stat[j][:, 0:1]).then_inc(act_step, 1)
                act.wait_ge(act_step, t * 3 + 1)
                nc.scalar.mul(stat[j][:, 1:2], stat[j][:, 0:1], -1.0 / GW).then_inc(act_step, 1)
                act.wait_ge(act_step, t * 3 + 2)
                act.wait_ge(gated, t - 1) if not (isinstance(t, int) and t < 1) else None
                nc.scalar.activation(ps[:, V, :], ps[:, V, :], ACT.Square, bias=stat[j][:, 1:2],
                                     accum_out=stat[j][:, 2:3]).then_inc(uv_read, 1)
                act.wait_ge(uv_read, t * 2 + 4)
                nc.scalar.mul(stat[j][:, 2:3], stat[j][:, 2:3], 1.0 / GW).then_inc(act_step, 1)

            def read_mix(t, j):
                sample = isinstance(t, int) and t == TILES - 1
                if sample:
                    act.wait_ge(normed, TILES)
                else:
                    act.wait_ge(mixed, t + 1)
                act.wait_ge(gated, t)
                for g in range(GROUPS):
                    c = slice(g * P, (g + 1) * P)
                    if sample:
                        op = nc.scalar.activation(mixb[:, c], vb[j][:, c], ACT.Identity, bias=b_sp[:, 1, g:g + 1],
                                                  scale=w00[:, g:g + 1])
                    else:
                        op = nc.scalar.activation(mixb[:, c], ps[:, MIX, c], ACT.Identity, bias=b_sp[:, 0, g:g + 1])
                    op.then_inc(biased, 1)

            def read_turned(t, j):
                act.wait_ge(gm_turned, t + 1)
                n = N_SAMPLE if isinstance(t, int) and t == TILES - 1 else P
                nc.scalar.copy(gmT[:, :, bass.ds(t * P, n)],
                               ps[:, TURN, :].rearrange("p (g q) -> p g q", q=P)[:, :, 0:n]).then_inc(gm_read, 1)

            staggered(act, TILES, [(0, read_uv), (1, read_mix), (2, read_turned)])
            with act.Fori(0, KC // 2) as i:
                for j in range(2):
                    for p, (c0, n) in enumerate(PIECES):
                        at = j * 3 + p
                        act.wait_ge(made_out[at % 2], i * 96 + at // 2 * 32)
                        for which in range(3):
                            wait_alone(act, gates_full, i * 18 + at * 3 + which + 1, idle[1])
                            src, to = ps[:, SETS[at % 2][which], 0:n], made[at % 2][:, which, 0:n]
                            if which < 2:
                                op = nc.scalar.activation(to, src, ACT.Sigmoid,
                                                          bias=gate_bias[:, which, bass.ds(i * 2 + j, 1)])
                            else:
                                op = nc.scalar.copy(to, src)
                            op.then_inc(gates_read, 1)

        @block.gpsimd
        def _(pool):
            pool.wait_ge(const_in, 16 * N_CONST)
            nc.gpsimd.affine_select(out=w_sp[:], in_=w_sp[:], compare_op=ALU.is_ge, fill=0.0, base=0,
                                    pattern=[[0, GROUPS], [1, P]], channel_multiplier=-1).then_inc(masked, 1)

            def normalise(t, j):
                step = Chain(pool, pool_step, t * 4)
                wait_alone(pool, act_step, t * 3 + 3, idle[2])
                step(nc.gpsimd.tensor_scalar(stat[j][:, 3:4], stat[j][:, 2:3], EPS, None, ALU.add))
                step(nc.gpsimd.tensor_tensor(stat[j][:, 3:4], stat[j][:, 3:4], minus_half[:], ALU.pow), wait=False)
                wait_alone(pool, pool_step, step.n, idle[2])
                step(nc.gpsimd.tensor_scalar(vb[j][:], vb[j][:], stat[j][:, 1:2], stat[j][:, 3:4], ALU.add, ALU.mult))
                step(nc.gpsimd.tensor_tensor(vb[j][:], vb[j][:], ln_v[:, 0, :], ALU.mult))
                nc.gpsimd.tensor_tensor(vb[j][:], vb[j][:], ln_v[:, 1, :], ALU.add).then_inc(normed, 1)

            def gate_u(t, j):
                pool.wait_ge(biased, t * GROUPS + GROUPS)
                nc.gpsimd.tensor_tensor(u[j][:], u[j][:], mixb[:], ALU.mult).then_inc(gated, 1)

            staggered(pool, TILES, [(0, normalise), (1, gate_u)])
            with pool.Fori(0, KC // 2) as i:
                for j in range(2):
                    for p, (c0, n) in enumerate(PIECES):
                        at = j * 3 + p
                        pool.wait_ge(gates_read, i * 18 + at * 3 + 9)
                        m = made[at % 2]
                        nc.gpsimd.tensor_tensor(m[:, 1, 0:n], m[:, 1, 0:n], m[:, 2, 0:n],
                                                ALU.mult).then_inc(multiplied, 1)

        @block.vector
        def _(dve):
            step = Chain(dve, taken)
            step(nc.vector.memset(top8[0][:], 0.0))
            step(nc.vector.memset(top8[1][:], 0.0))
            mine = [score_s[:, :]] + [score[t][:] for t in range(TOPK // P, NT)]
            for group in ((0, 6), (1, 5), (2, 4), (3,)):
                m = len(group)
                with dve.Fori(0, ROUNDS) as r:
                    for k, g in enumerate(group):
                        wait_alone(dve, taken, r * (2 * m) + (step.n - m + k + 1), idle[0])
                        nc.vector.max(top8[k][0:mine[g].shape[0], :], mine[g]).then_inc(taken, 1)
                    for k, g in enumerate(group):
                        wait_alone(dve, taken, r * (2 * m) + (step.n + k + 1), idle[0])
                        nc.vector.match_replace(mine[g], top8[k][0:mine[g].shape[0], :], mine[g],
                                                TAKEN).then_inc(taken, 1)
                step.n += 2 * m * ROUNDS
                for k, g in enumerate(group):
                    dve.wait_ge(taken, step.n)
                    if g > 0:
                        step(nc.vector.tensor_scalar(mine[g], mine[g], 2.0 * HIDDEN, NEG, ALU.is_gt, ALU.mult))
            own = score_s[:, PAST:PAST + 1]
            cached = score_s[:, 0:PAST]
            step(nc.vector.tensor_scalar(score_s[:], score_s[:], 2.0 * HIDDEN, None, ALU.is_lt))
            dve.wait_ge(gates_full, KC * 9)
            step(nc.vector.tensor_tensor_scan(counted, cached, cached, 0.0, ALU.add, ALU.max))
            nc.vector.scalar_tensor_tensor(cached, counted, own, cached, ALU.add, ALU.mult).then_inc(placed, 1)
            dve.wait_ge(const_in, 16 * N_CONST)
            step(nc.vector.tensor_copy(rank_b[:], rank[:]))
            by = pages_i[:].rearrange("p (two i g) -> p i two g", two=2, g=PAGES)
            step(nc.vector.tensor_copy(ids[:, :, :, 0].rearrange("p (i two) g -> p i two g", two=2), by))
            step(nc.vector.tensor_scalar(ids[:, :, :, 1], ids[:, :, :, 0], 0.0, part[:], ALU.mult, ALU.add))
            dve.wait_ge(place_turned, 1)
            step(nc.vector.tensor_copy(place[:], ps[:, MIX, 0:P].rearrange("p (g b) -> p g b", b=N_SAMPLE)))
            step(nc.vector.tensor_copy(keep["own_taken"][:], ps[0:1, MIX, 256:256 + N_SAMPLE]))
            dve.sem_inc(hot_used, 2)
            with dve.Fori(0, N_SAMPLE // 2) as i:
                for j in range(2):
                    b = i * 2 + j
                    dve.wait_ge(hot_used, b + 1)
                    for g in range(PAGES):
                        last = nc.vector.tensor_scalar(hot[j][:, g, :], rank_b[:], place[:, g, bass.ds(b, 1)], None,
                                                       ALU.is_equal)
                    last.then_inc(hot_ready, 1)
            dve.wait_ge(hot_used, N_SAMPLE + 2)
            step(nc.vector.tensor_copy(found[:], ps[:, TURN, 0:4 * N_SAMPLE].rearrange("p (n c) -> p n c", c=2)))
            step(nc.vector.scalar_tensor_tensor(rows_f[:], found[:, :, 0], float(P), found[:, :, 1], ALU.mult, ALU.add))
            step(nc.vector.tensor_copy(keep["rows"][:], rows_f[:]))


def attend(nc, ins, outs, keep, scratch):
    SCALE = HD ** -0.5
    with nc.cleanup_on_exit(), ExitStack() as ctx:
        def sb(name, shape, dt=F32):
            return ctx.enter_context(nc.sbuf_tensor(name, shape, dt))

        def sem(name):
            return nc.alloc_semaphore(name)

        ident, qT, kT, v, attnT = (keep[n] for n in ("ident", "qT", "kT", "v", "attnT"))
        masks = keep["score"]
        own_taken, rows = keep["own_taken"], keep["rows"]
        k_sel = sb("k_sel", [P, 2 * N_SAMPLE, AW])
        v_sel = sb("v_sel", [P, 2 * N_SAMPLE, AW])
        first = sb("first_masks", [P, 3 * P])
        probs = [sb(f"probs{j}", [P, SEQ]) for j in range(2)]
        probsT = [sb(f"probsT{j}", [P, SEQ]) for j in range(2)]
        top = [sb(f"top{j}", [P, 2]) for j in range(2)]
        total = [sb(f"total{j}", [P, HEADS]) for j in range(2)]
        out = sb("attn_rows", [P, AW])
        own_f = sb("own_f", [1, N_SAMPLE])
        own_b = sb("own_b", [1, N_SAMPLE], I32)
        own_row = sb("own_row", [2, N_SAMPLE], U32)
        lg = sb("lg", [P, 2, N_SAMPLE * HEADS])
        prob_s = sb("prob_s", [N_SAMPLE * HEADS, TOPK])
        stat_s = sb("stat_s", [N_SAMPLE * HEADS, 4])
        probT_s = sb("probT_s", [P, 2, N_SAMPLE * HEADS])
        ps = ctx.enter_context(nc.psum_tensor("ps_attn", [P, 8, 512], F32))
        OUT = 7

        const_in, own_in = sem("a_const_in"), sem("own_in")
        gathered = sem("gathered")
        own_ready = sem("own_ready")
        logits = sem("logits")
        masked = sem("masked")
        exped = sem("exped")
        turned = sem("turned")
        read_by = {"dve": sem("chunk_read_dve"), "act": sem("chunk_read_act")}
        weighted = sem("weighted")
        dve_step = sem("a_dve_step")
        out_ready = sem("out_ready")
        q_spread = sem("q_spread")
        lg_ready = sem("lg_ready")
        lg_turned, s_exped, p_ready, p_turned, pT_ready, s_out = (
            sem(n) for n in ("lg_turned", "s_exped", "p_ready", "p_turned", "pT_ready", "s_out"))
        units = [(t, h) for t in range(NT) for h in range(HEADS)]

        chunks, chunk_of = [], {}
        for s in range(len(units) + 2):
            if 0 <= s - 1 < len(units):
                blocks = units[s - 1][0] + 1
                for c in range(0, blocks, 4):
                    chunk_of["p", s - 1, c // 4] = len(chunks)
                    chunks.append(min(4, blocks - c))
            if s - 3 >= 0 and units[s - 3][1] == HEADS - 1:
                chunk_of["o", units[s - 3][0], 0] = len(chunks)
                chunks.append(4)
        chunk_of["o", NT - 1, 0] = len(chunks)
        chunks.append(4)
        reader = ["act" if n % 2 else "dve" for n in range(len(chunks))]
        for (kind, _, _), n in chunk_of.items():
            if kind == "o":
                reader[n] = "act"
        reads = [reader[:n + 1].count(reader[n]) for n in range(len(chunks))]

        def wait_read(eng, n):
            eng.wait_ge(read_by[reader[n]], reads[n])

        block = ctx.enter_context(nc.Block())

        @block.sync
        def _(sp):
            sp.dma_start(first[:], ins["first_masks"]).then_inc(const_in, 16)
            sp.dma_start(own_b[:], ins["rank"][:, 0:N_SAMPLE]).then_inc(own_in, 16)

        @block.gpsimd
        def _(pool):
            for to, pool_name in ((k_sel, "cache_k"), (v_sel, "cache_v")):
                for c in range(2 * N_SAMPLE):
                    pool.indirect_dma_start(out=to[:, c, :], out_offset=None, in_=ins[pool_name],
                                            in_offset=bass.IndirectOffsetOnAxis(ap=rows[:, c:c + 1], axis=0)
                                            ).then_inc(gathered, 16)
            pool.wait_ge(own_ready, 1)
            pool.wait_ge(gathered, 16 * 4 * N_SAMPLE)
            for to, name in ((k_sel, "k_all"), (v_sel, "v_all")):
                for b in range(N_SAMPLE):
                    pool.indirect_dma_start(out=to[0:2, 2 * b, :], out_offset=None, in_=outs[name].rearrange("t p n -> (t p) n"),
                                            in_offset=bass.IndirectOffsetOnAxis(ap=own_row[:, b:b + 1], axis=0),
                                            bounds_check=TOK - 1, oob_is_err=False).then_inc(gathered, 16)
            pool.wait_ge(gathered, 16 * 6 * N_SAMPLE)

        @block.tensor
        def _(pe):
            def make_logits(n):
                t, h = units[n]
                if n >= 2:
                    pe.wait_ge(masked, 2 * (n - 2) + 1)
                half, width = (h % 2) * HD, (t + 1) * P
                for c in range(0, width, 512):
                    c1 = min(width, c + 512)
                    mm = nc.tensor.matmul(ps[:, 2 * (n % 2) + c // 512, 0:c1 - c],
                                          qT[half:half + HD, h // 2, t * P:(t + 1) * P],
                                          kT[half:half + HD, h // 2, c:c1], start=True, stop=True)
                mm.then_inc(logits, 1)

            def turn(key, src, pieces):
                n = chunk_of[key]
                if n >= 3:
                    wait_read(pe, n - 3)
                for i in range(pieces):
                    mm = nc.tensor.transpose(ps[:, 4 + n % 3, i * P:(i + 1) * P], src[:, i * P:(i + 1) * P], ident[:])
                mm.then_inc(turned, 1)

            def turn_probs(n):
                t = units[n][0]
                pe.wait_ge(exped, n + 1)
                for c in range(0, t + 1, 4):
                    turn(("p", n, c // 4), probs[n % 2][:, c * P:], min(4, t + 1 - c))

            def weigh(n):
                t, h = units[n]
                if h == 0 and t > 0:
                    pe.wait_ge(out_ready, t)
                for c in range(t + 1):
                    if c % 4 == 0:
                        wait_read(pe, chunk_of["p", n, c // 4])
                    mm = nc.tensor.matmul(ps[:, OUT, h * HD:(h + 1) * HD], probsT[n % 2][:, c * P:(c + 1) * P],
                                          v[:, c, h * HD:(h + 1) * HD], start=(c == 0), stop=(c == t))
                mm.then_inc(weighted, 1)

            def turn_out(t):
                pe.wait_ge(out_ready, t + 1)
                turn(("o", t, 0), out, 4)

            for s in range(len(units) + 2):
                if s < len(units):
                    make_logits(s)
                if 0 <= s - 1 < len(units):
                    turn_probs(s - 1)
                if s - 3 >= 0 and units[s - 3][1] == HEADS - 1:
                    turn_out(units[s - 3][0])
                if s >= 2:
                    weigh(s - 2)
            turn_out(NT - 1)
            pe.wait_ge(masked, 2 * len(units))
            for b in range(N_SAMPLE):
                if b >= 2:
                    pe.wait_ge(lg_ready, b - 1)
                for k in range(AW // P):
                    mm = nc.tensor.matmul(ps[:, b % 2, k * P:(k + 1) * P],
                                          qT[:, k, SEQ + b:SEQ + b + 1].to_broadcast([P, P]), ident[:],
                                          start=True, stop=True)
                mm.then_inc(q_spread, 1)
            pe.wait_ge(lg_ready, N_SAMPLE)
            for half in range(2):
                mm = nc.tensor.transpose(ps[0:N_SAMPLE * HEADS, 2, half * P:(half + 1) * P], lg[:, half, :], ident[:])
            mm.then_inc(lg_turned, 1)
            pe.wait_ge(p_ready, 1)
            n = N_SAMPLE * HEADS
            for half in range(2):
                mm = nc.tensor.transpose(ps[:, 3, half * n:(half + 1) * n], prob_s[:, half * P:(half + 1) * P],
                                         ident[0:n, 0:n])
            mm.then_inc(p_turned, 1)
            pe.wait_ge(pT_ready, 1)
            pe.wait_ge(gathered, 16 * 6 * N_SAMPLE)
            for k in range(AW // P):
                for b in range(N_SAMPLE):
                    for half in range(2):
                        mm = nc.tensor.matmul(ps[:, 0, k * n + b * HEADS:k * n + (b + 1) * HEADS],
                                              v_sel[:, 2 * b + half, k * P:(k + 1) * P],
                                              probT_s[:, half, b * HEADS:(b + 1) * HEADS],
                                              start=(half == 0), stop=(half == 1))
            mm.then_inc(s_out, 1)

        def read_chunk(eng, copy, key, to):
            n = chunk_of[key]
            eng.wait_ge(turned, n + 1)
            copy(to, ps[:, 4 + n % 3, 0:chunks[n] * P]).then_inc(read_by[reader[n]], 1)

        def read_probs(eng, copy, who, n):
            t = units[n][0]
            for c in range(0, t + 1, 4):
                if reader[chunk_of["p", n, c // 4]] == who:
                    if n >= 2:
                        eng.wait_ge(weighted, n - 1)
                    read_chunk(eng, copy, ("p", n, c // 4), probsT[n % 2][:, c * P:min(t + 1, c + 4) * P])

        @block.scalar
        def _(act):
            for s in range(len(units) + 3):
                if s < len(units):
                    t, h = units[s]
                    act.wait_ge(masked, 2 * s + 2)
                    if h == 0 and t >= 2:
                        act.wait_ge(out_ready, t - 1)
                    row = probs[s % 2][:, 0:(t + 1) * P]
                    nc.scalar.activation(row, row, ACT.Exp, bias=top[s % 2][:, 1:2],
                                         accum_out=total[t % 2][:, h:h + 1]).then_inc(exped, 1)
                if 0 <= s - 1 < len(units):
                    read_probs(act, nc.scalar.copy, "act", s - 1)
                if s - 3 >= 0 and units[s - 3][1] == HEADS - 1:
                    t = units[s - 3][0]
                    n = chunk_of["o", t, 0]
                    act.wait_ge(turned, n + 1)
                    nc.scalar.copy(attnT[:, :, t * P:(t + 1) * P],
                                   ps[:, 4 + n % 3, :].rearrange("p (k q) -> p k q", q=P)).then_inc(read_by["act"], 1)
            act.wait_ge(lg_ready, N_SAMPLE + 2)
            nc.scalar.activation(prob_s[:], ps[0:N_SAMPLE * HEADS, 2, 0:TOPK], ACT.Exp, bias=stat_s[:, 1:2],
                                 scale=SCALE, accum_out=stat_s[:, 2:3]).then_inc(s_exped, 1)

        @block.vector
        def _(dve):
            step = Chain(dve, dve_step)
            step(nc.vector.memset(own_row[:], 1 << 20))
            step(nc.vector.tensor_scalar(own_f[:], own_taken[:], -float(1 << 20), float((1 << 20) + SEQ - 1), ALU.mult, ALU.add))
            dve.wait_ge(own_in, 16)
            nc.vector.tensor_tensor(own_row[0:1, :], own_f[:], own_b[:], ALU.add).then_inc(own_ready, 1)
            dve.wait_ge(const_in, 16)
            for s in range(len(units) + 2):
                if s < len(units):
                    t, h = units[s]
                    row = probs[s % 2][:, 0:(t + 1) * P]
                    banks = ps[:, 2 * (s % 2):2 * (s % 2) + 2, :].rearrange("p b c -> p (b c)")[:, 0:(t + 1) * P]
                    mask = masks[t][:] if t >= TOPK // P else first[:, t * P:t * P + (t + 1) * P]
                    dve.wait_ge(logits, s + 1)
                    if s >= 2:
                        dve.wait_ge(turned, chunk_of["p", s - 2, units[s - 2][0] // 4] + 1)
                    nc.vector.tensor_tensor_reduce(row, banks, mask, SCALE, -3.0e38, ALU.add, ALU.max,
                                                   top[s % 2][:, 0:1]).then_inc(masked, 1)
                    dve.wait_ge(masked, 2 * s + 1)
                    nc.vector.tensor_scalar(top[s % 2][:, 1:2], top[s % 2][:, 0:1], -1.0, None, ALU.mult).then_inc(masked, 1)
                if 0 <= s - 1 < len(units):
                    read_probs(dve, nc.vector.tensor_copy, "dve", s - 1)
                if s >= 2 and units[s - 2][1] == HEADS - 1:
                    t = units[s - 2][0]
                    dve.wait_ge(exped, s - 1)
                    step(nc.vector.reciprocal(total[t % 2][:], total[t % 2][:]))
                    dve.wait_ge(weighted, s - 1)
                    if t > 0:
                        wait_read(dve, chunk_of["o", t - 1, 0])
                    nc.vector.tensor_tensor(out[:].rearrange("p (h d) -> p h d", d=HD),
                                            ps[:, OUT, :].rearrange("p (h d) -> p h d", d=HD),
                                            total[t % 2][:].unsqueeze(2).to_broadcast([P, HEADS, HD]),
                                            ALU.mult).then_inc(out_ready, 1)
            dve.wait_ge(gathered, 16 * 6 * N_SAMPLE)
            dve.wait_ge(turned, len(chunks))
            for b in range(N_SAMPLE):
                dve.wait_ge(q_spread, b + 1)
                for half in range(2):
                    product = probs[half][:, 0:AW]
                    step(nc.vector.tensor_tensor(product, k_sel[:, 2 * b + half, :], ps[:, b % 2, :], ALU.mult))
                    last = nc.vector.tensor_reduce(lg[:, half, b * HEADS:(b + 1) * HEADS],
                                                   product.rearrange("p (h d) -> p h d", d=HD), AX.X, ALU.add)
                last.then_inc(lg_ready, 1)
            dve.wait_ge(lg_turned, 1)
            n = N_SAMPLE * HEADS
            nc.vector.tensor_reduce(stat_s[:, 0:1], ps[0:n, 2, 0:TOPK], AX.X, ALU.max).then_inc(lg_ready, 1)
            dve.wait_ge(lg_ready, N_SAMPLE + 1)
            nc.vector.tensor_scalar(stat_s[:, 1:2], stat_s[:, 0:1], -SCALE, None, ALU.mult).then_inc(lg_ready, 1)
            dve.wait_ge(s_exped, 1)
            step(nc.vector.reciprocal(stat_s[:, 3:4], stat_s[:, 2:3]))
            nc.vector.tensor_scalar(prob_s[:], prob_s[:], stat_s[:, 3:4], None, ALU.mult).then_inc(p_ready, 1)
            dve.wait_ge(p_turned, 1)
            nc.vector.tensor_copy(probT_s[:], ps[:, 3, 0:2 * n].rearrange("p (a c) -> p a c", a=2)).then_inc(pT_ready, 1)
            dve.wait_ge(s_out, 1)
            for k in range(AW // P):
                for odd in range(2):
                    q0 = odd * HD
                    mine = ps[q0:q0 + HD, 0, k * n:(k + 1) * n].rearrange("p (b h) -> p b h", h=HEADS)
                    nc.vector.tensor_copy(attnT[q0:q0 + HD, k, SEQ:SEQ + N_SAMPLE], mine[:, :, 2 * k + odd])


N_EXPERTS = 32
N_GROUPS = 4
PER_GROUP = N_EXPERTS // N_GROUPS
F = 256
SLOTS = TOK * N_EXPERTS
NOWHERE = float(1 << 20)
ROUTER = N_GROUPS + N_EXPERTS


def merge_and_route(nc, ins, outs, keep, scratch):
    with nc.cleanup_on_exit(), ExitStack() as ctx:
        def sb(name, shape, dt=F32):
            return ctx.enter_context(nc.sbuf_tensor(name, shape, dt))

        def sem(name):
            return nc.alloc_semaphore(name)

        ident, attnT, logits = keep["ident"], keep["attnT"], keep["router_logits"]
        KA = AW // P
        w_a = sb("w_a", [P, KA, D])
        w_o = sb("w_o", [P, KC, D])
        w_r = sb("w_r", [P, KC, ROUTER])
        ln1 = sb("ln1", [P, 2, D])
        b_r = sb("b_r", [P, ROUTER])
        minus_half = sb("minus_half1", [P, 1])
        mergedT = sb("mergedT", [P, KC, TOK])
        gates = [sb(f"gates{j}", [P, 2, 512]) for j in range(3)]
        x = [sb(f"x_rows{j}", [P, D]) for j in range(2)]
        h = [sb(f"h{j}", [P, D]) for j in range(2)]
        hT = sb("hT", [P, KC, P])
        stats = sb("stats1", [P, 2, 6])
        mv = [sb(f"mv{j}", [P, 2]) for j in range(2)]
        empty = sb("empty", [P, SLOTS // P], U32)
        ps = ctx.enter_context(nc.psum_tensor("ps_merge", [P, 8, 512], F32))

        w_a_in, w_o_in, const_in = sem("w_a_in"), sem("w_o_in"), sem("m_const_in")
        gates_in = [sem(f"gates_in{j}") for j in range(3)]
        x_in = [sem(f"x_rows_in{j}") for j in range(2)]
        branch = sem("branch")
        merged = sem("merged")
        list_emptied, rows_zeroed = sem("m_list_emptied"), sem("m_rows_zeroed")
        projected = sem("projected")
        added = sem("added")
        measured = sem("measured")
        powed = sem("powed")
        h_ready = sem("h_ready")
        h_out = [sem(f"h_out{j}") for j in range(2)]
        h_turned = sem("h_turned")
        hT_read = sem("hT_read")
        routed = sem("routed")
        logits_read = sem("logits_read")
        list_out = sem("list_out")
        dve_step = sem("m_dve_step")
        units = [(blk, p) for p in range(len(PIECES)) for blk in range(KC)]

        block = ctx.enter_context(nc.Block())

        @block.sync
        def _(sp):
            def load_gates(n):
                blk, p = units[n]
                c0, width = PIECES[p]
                for which, name in ((0, "gate_a"), (1, "merged_b")):
                    sp.dma_start(gates[n % 3][:, which, 0:width],
                                 scratch[name][blk, :, c0:c0 + width]).then_inc(gates_in[n % 3], 16)

            sp.dma_start(w_a[:], ins["w_a"]).then_inc(w_a_in, 16)
            for n in range(3):
                load_gates(n)
            sp.dma_start(w_o[:], ins["w_o"]).then_inc(w_o_in, 16)
            sp.dma_start(w_r[:], ins["w_router"]).then_inc(w_o_in, 16)
            for to, name in ((ln1[:, 0, :], "ln1_g"), (ln1[:, 1, :], "ln1_b"), (b_r[:], "b_router"),
                             (minus_half[:], "minus_half")):
                src = ins[name]
                sp.dma_start(to, src.to_broadcast([P, src.shape[1]]) if src.shape[0] == 1 else src).then_inc(const_in, 16)
            for j in range(2):
                sp.dma_start(x[j][:], ins["x_rows"][j]).then_inc(x_in[j], 16)
            for n in range(3, len(units)):
                sp.wait_ge(merged, 2 * (n - 3) + 2)
                load_gates(n)
            for j in range(2):
                sp.dma_start(keep["w_gate_up"][j][:], ins["w_gate_up"][j]).then_inc(keep["w_in"][j], 16)
                sp.dma_start(keep["w_down"][j][:], ins["w_down"][j]).then_inc(keep["w_in"][j], 16)
            for t in range(TILES):
                sp.wait_ge(h_ready, t + 1)
                sp.dma_start(scratch["h"][t], h[t % 2][:]).then_inc(h_out[t % 2], 16)
                if t + 2 < TILES:
                    sp.dma_start(x[t % 2][:], ins["x_rows"][t + 2]).then_inc(x_in[t % 2], 16)
            for j in range(2):
                sp.wait_ge(h_out[j], 16 * len(range(j, TILES, 2)))

        @block.gpsimd
        def _(pool):
            nc.gpsimd.memset(empty[:], 2 * TOK).then_inc(list_emptied, 1)
            pool.wait_ge(list_emptied, 1)
            pool.dma_start(scratch["list_of"].rearrange("(p n) o -> p (n o)", p=P), empty[:]).then_inc(list_out, 16)
            pool.wait_ge(const_in, 64)
            for t in range(TILES):
                pool.wait_ge(measured, t + 1)
                var = mv[t % 2][:, 1:2]
                nc.gpsimd.tensor_tensor(var, var, minus_half[:], ALU.pow).then_inc(powed, 1)
            pool.wait_ge(list_out, 16)

        @block.tensor
        def _(pe):
            pe.wait_ge(w_a_in, 16)
            for n, (blk, p) in enumerate(units):
                c0, width = PIECES[p]
                if n >= 3:
                    pe.wait_ge(merged, 2 * (n - 3) + 1)
                for k in range(KA):
                    mm = nc.tensor.matmul(ps[:, 3 + n % 3, 0:width], w_a[:, k, blk * P:(blk + 1) * P],
                                          attnT[:, k, c0:c0 + width], start=(k == 0), stop=(k == KA - 1))
                mm.then_inc(branch, 1)

            def project(t):
                if t >= 1:
                    pe.wait_ge(added, 2 * t)
                for c in range(2):
                    for k in range(KC):
                        mm = nc.tensor.matmul(ps[:, c, :], mergedT[:, k, t * P:(t + 1) * P],
                                              w_o[:, k, c * 512:(c + 1) * 512], start=(k == 0), stop=(k == KC - 1))
                mm.then_inc(projected, 1)

            def route(t):
                pe.wait_ge(h_ready, t + 1)
                for c in range(2):
                    if t >= 1:
                        pe.wait_ge(hT_read, 2 * (t - 1) + c + 1)
                    for k in range(4):
                        b = c * 4 + k
                        mm = nc.tensor.transpose(ps[:, 6 + c, k * P:(k + 1) * P], h[t % 2][:, b * P:(b + 1) * P], ident[:])
                    mm.then_inc(h_turned, 1)
                pe.wait_ge(hT_read, 2 * t + 2)
                if t >= 1:
                    pe.wait_ge(logits_read, t)
                for k in range(KC):
                    mm = nc.tensor.matmul(ps[:, 2, 0:ROUTER], hT[:, k, :], w_r[:, k, :], start=(k == 0), stop=(k == KC - 1))
                mm.then_inc(routed, 1)

            pe.wait_ge(merged, 2 * len(units))
            pe.wait_ge(rows_zeroed, 1)
            pe.wait_ge(w_o_in, 32)
            for t in range(TILES + 1):
                if t < TILES:
                    project(t)
                if t >= 1:
                    route(t - 1)

        @block.scalar
        def _(act):
            for t in range(TILES):
                for c in range(2):
                    act.wait_ge(h_turned, 2 * t + c + 1)
                    if t >= 1:
                        act.wait_ge(routed, t)
                    nc.scalar.copy(hT[:, c * 4:(c + 1) * 4, :],
                                   ps[:, 6 + c, :].rearrange("p (k q) -> p k q", q=P)).then_inc(hT_read, 1)

        @block.vector
        def _(dve):
            step = Chain(dve, dve_step)
            nc.vector.memset(mergedT[:, :, SEQ + N_SAMPLE:TOK], 0.0).then_inc(rows_zeroed, 1)
            for n, (blk, p) in enumerate(units):
                c0, width = PIECES[p]
                to = mergedT[:, blk, c0:c0 + width]
                dve.wait_ge(branch, n + 1)
                dve.wait_ge(gates_in[n % 3], 32 * (n // 3 + 1))
                nc.vector.tensor_tensor(to, ps[:, 3 + n % 3, 0:width], gates[n % 3][:, 0, 0:width],
                                        ALU.mult).then_inc(merged, 1)
                dve.wait_ge(merged, 2 * n + 1)
                nc.vector.tensor_tensor(to, to, gates[n % 3][:, 1, 0:width], ALU.add).then_inc(merged, 1)
            dve.wait_ge(const_in, 64)
            for t in range(TILES + 1):
                if t < TILES:
                    hb, m = h[t % 2], mv[t % 2]
                    dve.wait_ge(projected, t + 1)
                    dve.wait_ge(x_in[t % 2], 16 * (t // 2 + 1))
                    if t >= 2:
                        dve.wait_ge(h_out[t % 2], 16 * (t // 2))
                        dve.wait_ge(h_turned, 2 * (t - 2) + 2)
                    for c in range(2):
                        cols = slice(c * 512, (c + 1) * 512)
                        nc.vector.scalar_tensor_tensor(hb[:, cols], x[t % 2][:, cols], ALPHA, ps[:, c, :],
                                                       ALU.mult, ALU.add).then_inc(added, 1)
                    dve.wait_ge(added, 2 * t + 2)
                    for c in range(2):
                        step(nc.vector.bn_stats(stats[:, c, :], hb[:, c * 512:(c + 1) * 512]), wait=(c == 1))
                    step(nc.vector.bn_aggr(m[:], stats[:].rearrange("p a b -> p (a b)")))
                    nc.vector.tensor_scalar(m[:, 1:2], m[:, 1:2], EPS, None, ALU.add).then_inc(measured, 1)
                if t >= 1:
                    dve.wait_ge(routed, t)
                    nc.vector.tensor_tensor(logits[:, t - 1, :], ps[:, 2, 0:ROUTER], b_r[:], ALU.add).then_inc(logits_read, 1)
                if t < TILES:
                    dve.wait_ge(powed, t + 1)
                    step(nc.vector.tensor_scalar(hb[:], hb[:], m[:, 0:1], m[:, 1:2], ALU.subtract, ALU.mult))
                    step(nc.vector.tensor_tensor(hb[:], hb[:], ln1[:, 0, :], ALU.mult))
                    nc.vector.tensor_tensor(hb[:], hb[:], ln1[:, 1, :], ALU.add).then_inc(h_ready, 1)


def dispatch(nc, ins, outs, keep, scratch):
    with nc.cleanup_on_exit(), ExitStack() as ctx:
        def sb(name, shape, dt=F32):
            return ctx.enter_context(nc.sbuf_tensor(name, shape, dt))

        def sem(name):
            return nc.alloc_semaphore(name)

        logits = keep["router_logits"]
        lg, le = logits[:, :, 0:N_GROUPS], logits[:, :, N_GROUPS:ROUTER]
        T1, T4, T32 = [P, TILES], [P, TILES, N_GROUPS], [P, TILES, N_EXPERTS]
        best, best2, sum_g, e2, den = (sb(n, T1) for n in ("best", "best2", "sum_g", "e2", "den"))
        mark = sb("mark", T1)
        g4, g4b = sb("g4", T4), sb("g4b", T4)
        a32, b32, first, second = (sb(n, T32) for n in ("a32", "b32", "first", "second"))
        before = sb("before", [P, TILES + 1, N_EXPERTS])
        slot = [sb(f"slot_f{n}", T1) for n in range(2)]
        slot_out = [sb(f"slot_out{n}", T1, U32) for n in range(2)]
        fall = sb("fall", [P, N_EXPERTS])
        expert = sb("expert", [P, N_EXPERTS])
        valid = sb("valid", T1)
        away = sb("away", T1)
        entry = sb("entry", [P, 2, TILES], U32)
        earlier = sb("earlier", [P, P])
        ones = sb("ones", [P, P])
        most = sb("most_all", [P, 1])
        ps = ctx.enter_context(nc.psum_tensor("ps_route", [P, 2, 512], F32))

        const_in, step_sem, exp_ready, exped = sem("d_const_in"), sem("d_step"), sem("exp_ready"), sem("d_exped")
        counted, slots_ready, listed = sem("counted"), sem("slots_ready"), sem("listed")
        before_ready = sem("before_ready")

        block = ctx.enter_context(nc.Block())

        @block.sync
        def _(sp):
            for to, name in ((fall, "fall"), (expert, "expert"), (valid, "valid"), (away, "away"), (entry, "entry"),
                             (earlier, "earlier")):
                src = ins[name]
                sp.dma_start(to[:], src.to_broadcast([P, src.shape[1]]) if src.shape[0] == 1 else src).then_inc(const_in, 16)
            sp.wait_ge(listed, 16 * 2 * TILES)

        @block.gpsimd
        def _(pool):
            pool.wait_ge(slots_ready, 2)
            for which in range(2):
                for t in range(TILES):
                    pool.indirect_dma_start(
                        out=scratch["list_of"],
                        out_offset=bass.IndirectOffsetOnAxis(ap=slot_out[which][:, t:t + 1], axis=0),
                        in_=entry[:, which, t:t + 1], in_offset=None,
                        bounds_check=SLOTS - 1, oob_is_err=False).then_inc(listed, 16)

        @block.tensor
        def _(pe):
            pe.wait_ge(before_ready, 1)
            flat = TILES * N_EXPERTS
            nc.tensor.matmul(ps[:, 0, 0:flat], earlier[:], a32[:].rearrange("p t e -> p (t e)"), start=True, stop=False)
            nc.tensor.matmul(ps[:, 0, 0:flat], ones[:], before[:, 0:TILES, :].rearrange("p t e -> p (t e)"),
                             start=False, stop=True).then_inc(counted, 1)
            nc.tensor.matmul(ps[:, 1, 0:N_EXPERTS], ones[:], before[:, TILES, :], start=True, stop=True).then_inc(counted, 1)

        @block.scalar
        def _(act):
            act.wait_ge(exp_ready, 1)
            nc.scalar.activation(g4b[:], g4b[:], ACT.Exp).then_inc(exped, 1)
            act.wait_ge(exp_ready, 2)
            nc.scalar.activation(e2[:], e2[:], ACT.Exp).then_inc(exped, 1)

        @block.vector
        def _(dve):
            step = Chain(dve, step_sem)
            V = nc.vector

            def over(x, n):
                return x[:].unsqueeze(2).to_broadcast([P, TILES, n])

            def only_first(out, x, highest, n, spare):
                weights = fall[:, N_EXPERTS - n:].unsqueeze(1).to_broadcast([P, TILES, n])
                step(V.tensor_reduce(highest[:], x, AX.X, ALU.max))
                step(V.tensor_tensor(spare, x, over(highest, n), ALU.is_equal))
                step(V.tensor_tensor(spare, spare, weights, ALU.mult))
                step(V.tensor_reduce(mark[:], spare, AX.X, ALU.max))
                step(V.tensor_tensor(out, spare, over(mark, n), ALU.is_equal))

            dve.wait_ge(const_in, 16 * 6)
            step(V.memset(ones[:], 1.0))
            only_first(g4[:], lg, best, N_GROUPS, a32[:, :, 0:N_GROUPS])
            V.tensor_tensor(g4b[:], lg, over(best, N_GROUPS), ALU.subtract).then_inc(exp_ready, 1)
            step(V.tensor_scalar(g4[:], g4[:], -1.0, 1.0e30, ALU.add, ALU.mult))
            step(V.tensor_tensor(b32[:].rearrange("p t (g e) -> p t g e", g=N_GROUPS), le.rearrange("p t (g e) -> p t g e", g=N_GROUPS),
                                 g4[:].unsqueeze(3).to_broadcast([P, TILES, N_GROUPS, PER_GROUP]), ALU.add))
            only_first(first[:], b32[:], best, N_EXPERTS, a32[:])
            step(V.scalar_tensor_tensor(b32[:], first[:], -3.0e30, b32[:], ALU.mult, ALU.add))
            only_first(second[:], b32[:], best2, N_EXPERTS, a32[:])
            V.tensor_tensor(e2[:], best2[:], best[:], ALU.subtract).then_inc(exp_ready, 1)
            step(V.tensor_tensor(a32[:], first[:], second[:], ALU.add))
            step(V.tensor_tensor(a32[:], a32[:], over(valid, N_EXPERTS), ALU.mult))
            step(V.memset(before[:, 0, :], 0.0))
            for t in range(TILES):
                last = V.tensor_tensor(before[:, t + 1, :], before[:, t, :], a32[:, t, :], ALU.add)
                if t < TILES - 1:
                    step(last)
            last.then_inc(before_ready, 1)
            dve.wait_ge(exped, 2)
            w = keep["weights"]
            step(V.tensor_reduce(sum_g[:], g4b[:], AX.X, ALU.add))
            step(V.tensor_scalar(den[:], e2[:], 1.0, None, ALU.add))
            step(V.tensor_tensor(den[:], den[:], sum_g[:], ALU.mult))
            step(V.reciprocal(w[:, 0, :], den[:]))
            step(V.tensor_tensor(w[:, 1, :], w[:, 0, :], e2[:], ALU.mult))
            dve.wait_ge(counted, 1)
            numbers = expert[:].unsqueeze(1).to_broadcast(T32)
            step(V.scalar_tensor_tensor(b32[:], ps[:, 0, 0:TILES * N_EXPERTS].rearrange("p (t e) -> p t e", e=N_EXPERTS),
                                        float(N_EXPERTS), numbers, ALU.mult, ALU.add))
            for which, choice in enumerate((first, second)):
                step(V.tensor_tensor(choice[:], choice[:], b32[:], ALU.mult))
                step(V.tensor_reduce(slot[which][:], choice[:], AX.X, ALU.add))
                V.tensor_tensor(slot_out[which][:], slot[which][:], away[:], ALU.add).then_inc(slots_ready, 1)
            dve.wait_ge(counted, 2)
            step(V.tensor_reduce(most[:], ps[:, 1, 0:N_EXPERTS], AX.X, ALU.max))
            step(V.tensor_copy(keep["most"][:], most[0:1, :]))


def read_lists(nc, keep, scratch, chunk, tag):
    with nc.cleanup_on_exit(), nc.sbuf_tensor(f"{tag}_wraps", [P, N_EXPERTS], F32) as wraps, nc.Block() as block:
        list_in, step_sem = nc.alloc_semaphore(f"{tag}_list_in"), nc.alloc_semaphore(f"{tag}_l_step")
        entries, tokens = keep["entries"], keep["tokens"]

        @block.sync
        def _(sp):
            lists = scratch["list_of"].rearrange("(c p e) o -> c p (e o)", p=P, e=N_EXPERTS)
            sp.dma_start(entries[:], lists[bass.ds(chunk, 1)]).then_inc(list_in, 16)

        @block.vector
        def _(dve):
            step = Chain(dve, step_sem)
            dve.wait_ge(list_in, 16)
            step(nc.vector.tensor_scalar(wraps[:], entries[:], float(TOK), -float(TOK), ALU.is_ge, ALU.mult))
            step(nc.vector.tensor_tensor(wraps[:], wraps[:], entries[:], ALU.add))
            step(nc.vector.tensor_scalar(tokens[:], wraps[:], float(TOK - 1), None, ALU.min))


def experts(nc, ins, keep, scratch, loaded, tag):
    with nc.cleanup_on_exit(), ExitStack() as ctx:
        def sb(name, shape, dt=F32):
            return ctx.enter_context(nc.sbuf_tensor(f"{tag}_{name}", shape, dt))

        def sem(name):
            return nc.alloc_semaphore(f"{tag}_{name}")

        ident, tokens, entries, w_gu, w_dn = (keep[n] for n in ("ident", "tokens", "entries", "w_gate_up", "w_down"))
        w_in = keep["w_in"] if loaded else [sem(f"w_in{j}") for j in range(2)]
        rows = [sb(f"e_rows{j}", [P, D]) for j in range(2)]
        rowsT = [sb(f"e_rowsT{j}", [P, KC, P]) for j in range(2)]
        hidden = [sb(f"hidden{j}", [P, F]) for j in range(2)]
        hiddenT = [sb(f"hiddenT{j}", [P, F // P, P]) for j in range(2)]
        result = [sb(f"result{j}", [P, D]) for j in range(2)]
        ps = ctx.enter_context(nc.psum_tensor(f"{tag}_ps_experts", [P, 8, 512], F32))
        GU, HT = 2, 3
        rows_in = [sem(f"e_rows_in{j}") for j in range(2)]
        rows_turned = sem("e_rows_turned")
        rowsT_act, rowsT_dve = sem("e_rowsT_act"), sem("e_rowsT_dve")
        gate_up = sem("e_gate_up")
        silu = sem("e_silu")
        hid = sem("e_hidden")
        hid_turned = sem("e_hid_turned")
        hidT_read = sem("e_hidT_read")
        down = sem("e_down")
        down_act, down_dve = sem("e_down_act"), sem("e_down_dve")
        stored = [sem(f"e_stored{j}") for j in range(2)]
        idle = [sem(f"e_idle{n}") for n in range(4)]

        block = ctx.enter_context(nc.Block())

        @block.sync
        def _(sp):
            def load(e, j):
                sp.dma_start(w_gu[j][:], ins["w_gate_up"][bass.ds(e, 1)]).then_inc(w_in[j], 16)
                sp.dma_start(w_dn[j][:], ins["w_down"][bass.ds(e, 1)]).then_inc(w_in[j], 16)

            if not loaded:
                for j in range(2):
                    load(j, j)
            with sp.Fori(1, N_EXPERTS // 2) as i:
                for j in range(2):
                    sp.wait_ge(down, (i * 2 + j) * 2 - 2)
                    load(i * 2 + j, j)

        @block.gpsimd
        def _(pool):
            for e in range(N_EXPERTS + 2):
                if e < N_EXPERTS:
                    if e >= 2:
                        pool.wait_ge(rows_turned, 2 * (e - 2) + 2)
                    pool.indirect_dma_start(out=rows[e % 2][:], out_offset=None, in_=scratch["h"].rearrange("t p n -> (t p) n"),
                                            in_offset=bass.IndirectOffsetOnAxis(ap=tokens[:, e:e + 1], axis=0)
                                            ).then_inc(rows_in[e % 2], 16)
                if e >= 2:
                    pool.wait_ge(down_act, e + 1)
                    pool.wait_ge(down_dve, e + 1)
                    pool.indirect_dma_start(out=scratch["pair_out"].rearrange("c n d -> (c n) d"),
                                            out_offset=bass.IndirectOffsetOnAxis(ap=entries[:, e - 2:e - 1], axis=0),
                                            in_=result[e % 2][:], in_offset=None,
                                            bounds_check=2 * TOK - 1, oob_is_err=False).then_inc(stored[e % 2], 16)
            for j in range(2):
                pool.wait_ge(stored[j], 16 * N_EXPERTS // 2)

        @block.tensor
        def _(pe):
            def make_hidden(e, j):
                pe.wait_ge(w_in[j], (e - j) * 16 + 32)
                pe.wait_ge(rowsT_act, e + 2)
                pe.wait_ge(rowsT_dve, e + 2)
                pe.wait_ge(hid, e + 1)
                for k in range(KC):
                    mm = nc.tensor.matmul(ps[:, GU, :], rowsT[j][:, k, :], w_gu[j][:, k, :], start=(k == 0), stop=(k == KC - 1))
                mm.then_inc(gate_up, 1)

            def turn_rows(e, j):
                pe.wait_ge(rows_in[j], (e - j) * 8 + 16)
                for c, read in enumerate((rowsT_act, rowsT_dve)):
                    pe.wait_ge(read, e + 1)
                    for k in range(4):
                        b = c * 4 + k
                        mm = nc.tensor.transpose(ps[:, c, k * P:(k + 1) * P], rows[j][:, b * P:(b + 1) * P], ident[:])
                    mm.then_inc(rows_turned, 1)

            def finish(e, j):
                pe.wait_ge(hid, e + 2)
                pe.wait_ge(hidT_read, e + 1)
                for k in range(F // P):
                    mm = nc.tensor.transpose(ps[:, HT, k * P:(k + 1) * P], hidden[j][:, k * P:(k + 1) * P], ident[:])
                mm.then_inc(hid_turned, 1)
                pe.wait_ge(hidT_read, e + 2)
                for c, read in enumerate((down_act, down_dve)):
                    pe.wait_ge(read, e + 1)
                    for k in range(F // P):
                        mm = nc.tensor.matmul(ps[:, 4 + 2 * j + c, :], hiddenT[j][:, k, :], w_dn[j][:, k, c * 512:(c + 1) * 512],
                                              start=(k == 0), stop=(k == F // P - 1))
                    mm.then_inc(down, 1)

            staggered(pe, N_EXPERTS, [(1, make_hidden), (0, turn_rows), (1, finish)])

        @block.scalar
        def _(act):
            act.sem_inc(rowsT_act, 1)
            act.sem_inc(hidT_read, 1)
            act.sem_inc(down_act, 2)

            def read_rows(e, j):
                act.wait_ge(rows_turned, e * 2 + 1)
                nc.scalar.copy(rowsT[j][:, 0:4, :], ps[:, 0, :].rearrange("p (k q) -> p k q", q=P)).then_inc(rowsT_act, 1)

            def do_silu(e, j):
                act.wait_ge(gate_up, e + 1)
                nc.scalar.activation(hidden[j][:], ps[:, GU, 0:F], ACT.Silu).then_inc(silu, 1)

            def read_rest(e, j):
                act.wait_ge(hid_turned, e + 1)
                nc.scalar.copy(hiddenT[j][:], ps[:, HT, 0:F].rearrange("p (k q) -> p k q", q=P)).then_inc(hidT_read, 1)
                act.wait_ge(down, e * 2 + 1)
                if isinstance(e, int) and e < 2:
                    pass
                else:
                    act.wait_ge(stored[j], (e - j) * 8)
                nc.scalar.copy(result[j][:, 0:512], ps[:, 4 + 2 * j, :]).then_inc(down_act, 1)

            staggered(act, N_EXPERTS, [(1, do_silu), (0, read_rows), (1, read_rest)])

        @block.vector
        def _(dve):
            dve.sem_inc(rowsT_dve, 1)
            dve.sem_inc(hid, 1)
            dve.sem_inc(down_dve, 2)

            def read_rows(e, j):
                dve.wait_ge(rows_turned, e * 2 + 2)
                nc.vector.tensor_copy(rowsT[j][:, 4:8, :], ps[:, 1, :].rearrange("p (k q) -> p k q", q=P)).then_inc(rowsT_dve, 1)

            def multiply(e, j):
                dve.wait_ge(silu, e + 1)
                nc.vector.tensor_tensor(hidden[j][:], hidden[j][:], ps[:, GU, F:2 * F], ALU.mult).then_inc(hid, 1)

            def read_down(e, j):
                dve.wait_ge(down, e * 2 + 2)
                if not isinstance(e, int) or e >= 2:
                    dve.wait_ge(stored[j], (e - j) * 8)
                nc.vector.tensor_copy(result[j][:, 512:D], ps[:, 5 + 2 * j, :]).then_inc(down_dve, 1)

            staggered(dve, N_EXPERTS, [(1, multiply), (0, read_rows), (1, read_down)])


def finish(nc, ins, outs, keep, scratch):
    with nc.cleanup_on_exit(), ExitStack() as ctx:
        def sb(name, shape, dt=F32):
            return ctx.enter_context(nc.sbuf_tensor(name, shape, dt))

        def sem(name):
            return nc.alloc_semaphore(name)

        weights = keep["weights"]
        h = [sb(f"f_h{j}", [P, D]) for j in range(BUFS)]
        part = [[sb(f"f_part{n}_{j}", [P, D]) for j in range(BUFS)] for n in range(2)]
        stats = sb("f_stats", [P, 2, 6])
        mv = [sb(f"f_mv{j}", [P, 2]) for j in range(BUFS)]
        ln2 = sb("ln2", [P, 2, D])
        minus_half = sb("minus_half2", [P, 1])
        const_in = sem("f_const_in")
        h_in = [sem(f"f_h_in{j}") for j in range(BUFS)]
        parts_in = [sem(f"f_parts_in{j}") for j in range(BUFS)]
        measured, powed, normed, scaled, y_ready = (sem(n) for n in ("f_measured", "f_powed", "f_normed", "f_scaled", "f_y"))
        y_out = [sem(f"y_out{j}") for j in range(BUFS)]
        dve_step = sem("f_dve_step")

        block = ctx.enter_context(nc.Block())

        @block.sync
        def _(sp):
            def load(t):
                j, n = t % BUFS, (P if t < NT else N_SAMPLE)
                sp.dma_start(h[j][:], scratch["h"][t]).then_inc(h_in[j], 16)
                for which in range(2):
                    sp.dma_start(part[which][j][0:n, :], scratch["pair_out"][which, t * P:t * P + n, :]).then_inc(parts_in[j], 16)

            for t in range(BUFS):
                load(t)
            for to, name in ((ln2[:, 0, :], "ln2_g"), (ln2[:, 1, :], "ln2_b"), (minus_half[:], "minus_half")):
                src = ins[name]
                sp.dma_start(to, src.to_broadcast([P, src.shape[1]]) if src.shape[0] == 1 else src).then_inc(const_in, 16)
            for t in range(TILES):
                j = t % BUFS
                sp.wait_ge(y_ready, t + 1)
                sp.dma_start(outs["y_all"][t], h[j][:]).then_inc(y_out[j], 16)
                if t + BUFS < TILES:
                    sp.wait_ge(y_out[j], 16 * (t // BUFS + 1))
                    load(t + BUFS)
            for j in range(BUFS):
                sp.wait_ge(y_out[j], 16 * TILES // BUFS)

        @block.gpsimd
        def _(pool):
            pool.wait_ge(const_in, 48)
            for t in range(TILES):
                j = t % BUFS
                pool.wait_ge(measured, t + 1)
                nc.gpsimd.tensor_tensor(mv[j][:, 1:2], mv[j][:, 1:2], minus_half[:], ALU.pow).then_inc(powed, 1)
                pool.wait_ge(normed, t + 1)
                nc.gpsimd.tensor_tensor(h[j][:], h[j][:], ln2[:, 0, :], ALU.mult).then_inc(scaled, 1)
                pool.wait_ge(scaled, t + 1)
                nc.gpsimd.tensor_tensor(h[j][:], h[j][:], ln2[:, 1, :], ALU.add).then_inc(y_ready, 1)

        @block.vector
        def _(dve):
            step = Chain(dve, dve_step)
            for t in range(TILES + 1):
                if t < TILES:
                    j = t % BUFS
                    dve.wait_ge(h_in[j], 16 * (t // BUFS + 1))
                    step(nc.vector.tensor_scalar(h[j][:], h[j][:], ALPHA, None, ALU.mult))
                    dve.wait_ge(parts_in[j], 32 * (t // BUFS + 1))
                    for n in range(2):
                        step(nc.vector.scalar_tensor_tensor(h[j][:], part[n][j][:], weights[:, n, t:t + 1], h[j][:],
                                                            ALU.mult, ALU.add))
                    for c in range(2):
                        step(nc.vector.bn_stats(stats[:, c, :], h[j][:, c * 512:(c + 1) * 512]), wait=(c == 1))
                    step(nc.vector.bn_aggr(mv[j][:], stats[:].rearrange("p a b -> p (a b)")))
                    nc.vector.tensor_scalar(mv[j][:, 1:2], mv[j][:, 1:2], EPS, None, ALU.add).then_inc(measured, 1)
                if t >= 1:
                    i = (t - 1) % BUFS
                    dve.wait_ge(powed, t)
                    nc.vector.tensor_scalar(h[i][:], h[i][:], mv[i][:, 0:1], mv[i][:, 1:2],
                                            ALU.subtract, ALU.mult).then_inc(normed, 1)


def rope_table():
    rot = 2 * ROT_HALF
    inv = np.power(np.float32(500000.0), -np.arange(0, rot, 2, dtype=np.float32) / np.float32(rot)).astype(np.float32)
    pos = np.concatenate([np.arange(SEQ), np.full(P, PAST)]).astype(np.float32)
    ang = (pos[:, None] * inv[None, :]).astype(np.float32).astype(np.float64)
    t = np.stack([np.cos(ang), np.sin(ang)], 1).astype(np.float32)
    return np.ascontiguousarray(t.reshape(TILES, P, 2, ROT_HALF).transpose(1, 0, 2, 3))


def build(nc, ins, outs, scratch):
    with ExitStack() as whole:
        def sb(name, shape, dt=F32, side="left", ctx=whole):
            return ctx.enter_context(nc.sbuf_tensor(name, shape, dt, side=side))

        keep = {"ident": sb("ident", [P, P])}
        with ExitStack() as mixer:
            for name, shape, dt in (("wi", [P, TILES, IDX_HEADS], F32), ("own_taken", [1, N_SAMPLE], F32),
                                    ("rows", [P, 2 * N_SAMPLE], U32), ("qT", [P, AW // P, TOK], F32),
                                    ("kT", [P, AW // P, TOK], F32), ("qkiT", [P, 3, TOK], F32),
                                    ("v", [P, TILES, AW], F32)):
                keep[name] = sb(name, shape, dt, ctx=mixer)
            with nc.sbuf_tensor("kidx", [P, N_SAMPLE // 2 * PAST], F32, side="right") as keep["kidx"], \
                    nc.sbuf_tensor("page_table", [1, N_SAMPLE * PAGES], I32, side="right") as keep["table"]:
                project(nc, ins, outs, keep)
                keep["score"] = [None] * (TOPK // P) + [sb(f"score{t}", [P, (t + 1) * P], ctx=mixer)
                                                        for t in range(TOPK // P, NT)]
                keep["score_s"] = sb("score_s", [N_SAMPLE, PAST + 1], ctx=mixer)
                index_scores(nc, ins, outs, keep)
            choose_keys_and_gate(nc, ins, outs, keep, scratch)
            keep["attnT"] = sb("attnT", [P, AW // P, SEQ + N_SAMPLE], side="right")
            attend(nc, ins, outs, keep, scratch)
        keep["w_gate_up"] = [sb(f"w_gate_up{j}", [P, KC, 2 * F], side="right") for j in range(2)]
        keep["w_down"] = [sb(f"w_down{j}", [P, F // P, D], side="right") for j in range(2)]
        keep["w_in"] = [whole.enter_context(nc.semaphore(f"w_in_expert{j}")) for j in range(2)]
        for name, shape, dt in (("router_logits", [P, TILES, ROUTER], F32), ("weights", [P, 2, TILES], F32),
                                ("entries", [P, N_EXPERTS], U32), ("tokens", [P, N_EXPERTS], U32), ("most", [1, 1], I32)):
            keep[name] = sb(name, shape, dt)
        merge_and_route(nc, ins, outs, keep, scratch)
        dispatch(nc, ins, outs, keep, scratch)
        read_lists(nc, keep, scratch, 0, "main")
        experts(nc, ins, keep, scratch, loaded=True, tag="main")
        longest = nc.values_load(keep["most"][:], min_val=0, max_val=TOK)
        with nc.If(longest > P):
            with nc.Fori(1, (longest + (P - 1)) // P) as chunk:
                read_lists(nc, keep, scratch, chunk, "rest")
                experts(nc, ins, keep, scratch, loaded=False, tag="rest")
        finish(nc, ins, outs, keep, scratch)


def layout(inp):
    x = np.zeros((TOK, D), np.float32)
    x[:SEQ] = inp["x_prompt"][0]
    x[SEQ:SEQ + N_SAMPLE] = inp["x_sample"][:, 0]
    w_in = np.asarray(inp["w_in"])
    a = {"x_tiles": x.T.reshape(KC, P, TILES, P).transpose(2, 1, 0, 3),
         "w_qkvi": w_in[:, :W_QKVI].reshape(KC, P, W_QKVI),
         "rot": rope_table(), "ident": np.eye(P, dtype=np.float32),
         "causal_cap": np.where(np.tri(P, dtype=bool), np.float32(3e38), np.float32(HIDDEN)).astype(np.float32),
         "page_table": np.asarray(inp["page_table"]).reshape(N_SAMPLE // 2, 2, PAGES).transpose(1, 0, 2).reshape(1, -1),
         "kidx_pool": np.asarray(inp["cache_kidx"]).transpose(0, 2, 1)}
    o = np.cumsum([0, AW, AW, AW, IDX_HEADS * HD, HD, IDX_HEADS, GW, GW, D, D])
    a["w_uv"] = w_in[:, o[6]:o[8]].reshape(KC, P, 2 * GW).transpose(1, 0, 2)
    by_block = [w_in[:, o[n]:o[n + 1]].reshape(KC, P, KC, P).transpose(2, 1, 0, 3) for n in (8, 9)]
    by_block.append(np.asarray(inp["w_branch_b"]).reshape(GROUPS, P, KC, P).transpose(2, 1, 0, 3))
    a["w_gate"] = np.concatenate(by_block, 2)
    a["x_all"] = x[:SEQ + N_SAMPLE].T.reshape(KC, P, -1).transpose(1, 0, 2)
    a["w_spatial_t"] = np.asarray(inp["w_spatial"]).transpose(2, 0, 1)
    a["w_spatial_00"] = np.asarray(inp["w_spatial"])[:, 0, 0].reshape(1, GROUPS)
    a["b_spatial_t"] = np.asarray(inp["b_spatial"]).T
    a["b_spatial_0"] = np.asarray(inp["b_spatial"])[:, 0].reshape(1, GROUPS)
    a["gate_bias_t"] = np.asarray(inp["gate_bias"]).reshape(2, KC, P).transpose(2, 0, 1)
    a["ln_v_g"], a["ln_v_b"] = (np.asarray(inp[n]).reshape(1, -1) for n in ("ln_v_g", "ln_v_b"))
    a["part_index"] = np.arange(P, dtype=np.float32).reshape(P, 1)
    a["minus_half"] = np.full((P, 1), -0.5, np.float32)
    a["rank"] = np.arange(1, TOPK + 1, dtype=np.int32).reshape(1, -1)
    tri = np.where(np.tri(P, dtype=bool), np.float32(0), np.float32(NEG)).astype(np.float32)
    a["first_masks"] = np.concatenate([tri, np.zeros((P, P), np.float32), tri], 1)
    for n in ("cache_k", "cache_v"):
        a[n] = np.asarray(inp[n]).reshape(-1, AW)
    a["x_rows"] = x.reshape(TILES, P, D)
    a["w_a"] = np.asarray(inp["w_branch_a"]).reshape(AW // P, P, D).transpose(1, 0, 2)
    a["w_o"] = np.asarray(inp["w_o"]).reshape(KC, P, D).transpose(1, 0, 2)
    router = [np.asarray(inp["w_router_group"])] + list(np.asarray(inp["w_router_expert"]))
    a["w_router"] = np.concatenate(router, 1).reshape(KC, P, ROUTER).transpose(1, 0, 2)
    a["b_router"] = np.concatenate([np.asarray(inp["b_router_group"]), np.asarray(inp["b_router_expert"]).ravel()]).reshape(1, -1)
    for n in ("ln1_g", "ln1_b", "ln2_g", "ln2_b"):
        a[n] = np.asarray(inp[n]).reshape(1, D)
    gate, up = (np.asarray(inp[n]).reshape(N_EXPERTS, KC, P, F) for n in ("w_expert_gate", "w_expert_up"))
    a["w_gate_up"] = np.concatenate([gate, up], 3).transpose(0, 2, 1, 3)
    a["w_down"] = np.asarray(inp["w_expert_down"]).reshape(N_EXPERTS, F // P, P, D).transpose(0, 2, 1, 3)
    number = np.arange(TOK).reshape(TILES, P).T
    a["fall"] = np.arange(N_EXPERTS, 0, -1, dtype=np.float32).reshape(1, -1)
    a["expert"] = np.arange(N_EXPERTS, dtype=np.float32).reshape(1, -1)
    a["valid"] = (number < SEQ + N_SAMPLE).astype(np.float32)
    a["away"] = np.where(number < SEQ + N_SAMPLE, np.float32(0), np.float32(NOWHERE))
    a["entry"] = np.stack([number, number + TOK], 1).astype(np.uint32)
    a["earlier"] = np.triu(np.ones((P, P), np.float32), 1)
    return {k: np.ascontiguousarray(v) for k, v in a.items()}


def kernel(**inputs):
    import concourse.bacc as bacc
    from concourse.bass_utils import run_bass_kernel_spmd

    nc = bacc.Bacc("TRN2", target_bir_lowering=False, num_devices=1)
    arrays = layout(inputs)
    ins = {k: nc.dram_tensor(f"in_{k}", list(v.shape), mybir.dt.from_np(v.dtype), kind="ExternalInput").ap()
           for k, v in arrays.items()}
    shapes = {"y_all": [TILES, P, D], "k_all": [TILES, P, AW], "v_all": [TILES, P, AW], "kidx_all": [TILES, P, HD],
              "chunk_v": [N_SAMPLE, GW]}
    outs = {k: nc.dram_tensor(f"out_{k}", v, F32, kind="ExternalOutput").ap() for k, v in shapes.items()}
    shapes = {"gate_a": [KC, P, SEQ + N_SAMPLE], "merged_b": [KC, P, SEQ + N_SAMPLE]}
    shapes |= {"h": [TILES, P, D], "pair_out": [2, TOK, D]}
    scratch = {k: nc.dram_tensor(k, v, F32, kind="Internal").ap() for k, v in shapes.items()}
    scratch["list_of"] = nc.dram_tensor("list_of", [SLOTS, 1], U32, kind="Internal").ap()
    build(nc, ins, outs, scratch)
    r = run_bass_kernel_spmd(nc, [{f"in_{k}": v for k, v in arrays.items()}], core_ids=[0]).results[0]
    y, k, v, ki = (np.asarray(r[f"out_{n}"]).reshape(TOK, -1) for n in ("y_all", "k_all", "v_all", "kidx_all"))
    s = slice(SEQ, SEQ + N_SAMPLE)
    return (y[:SEQ].reshape(1, SEQ, D), y[s].reshape(N_SAMPLE, 1, D),
            k[:SEQ].reshape(1, SEQ, HEADS, HD), v[:SEQ].reshape(1, SEQ, HEADS, HD), ki[:SEQ].reshape(1, SEQ, HD),
            k[s].reshape(N_SAMPLE, 1, HEADS, HD), v[s].reshape(N_SAMPLE, 1, HEADS, HD),
            ki[s].reshape(N_SAMPLE, 1, HD), np.asarray(r["out_chunk_v"]).reshape(N_SAMPLE, 1, GW))
```
